# Optimizing a Trainium2 kernel written in Bass

```python
import math
import jax, jax.numpy as jnp
from jax import lax
import numpy as np

D_MODEL = 2048
BATCH = 1
SEQ = 512
DEPTH = 1

GDN_HEADS = 8
GDN_DK = 128
GDN_DV = 128
GDN_CONV = 4
GDN_CHUNK = 64
GDN_KEY_W = GDN_HEADS * GDN_DK
GDN_VAL_W = GDN_HEADS * GDN_DV
GDN_QKV_W = 2 * GDN_KEY_W + GDN_VAL_W
MLA_HEADS = 8
MLA_Q_RANK = 512
MLA_KV_RANK = 256
MLA_NOPE = 128
MLA_ROPE = 64
MLA_V = 128
MLA_QK = MLA_NOPE + MLA_ROPE
MLA_VAL_W = MLA_HEADS * MLA_V
ROPE_THETA = 10000.0
Q_BLOCK = 128
NORM_EPS = 1e-6
POS_OFFSET_MAX = 1024

IN_WIDTHS = (
    GDN_QKV_W,
    GDN_VAL_W,
    GDN_HEADS,
    GDN_HEADS,
    MLA_Q_RANK,
    MLA_KV_RANK,
    MLA_ROPE,
    MLA_VAL_W,
    D_MODEL,
    D_MODEL,
)
D_IN = GDN_QKV_W + GDN_VAL_W + 2 * GDN_HEADS + MLA_Q_RANK + MLA_KV_RANK + MLA_ROPE + MLA_VAL_W + 2 * D_MODEL

kernel_name = "gated_deltanet_mla_parallel_hybrid"

def rms_norm(x, w):
    xf = x.astype(jnp.float32)
    y = xf * lax.rsqrt(jnp.mean(xf * xf, axis=-1, keepdims=True) + NORM_EPS)
    return (y * w.astype(jnp.float32)).astype(x.dtype)

def l2_norm(x):
    xf = x.astype(jnp.float32)
    return (xf * lax.rsqrt(jnp.sum(xf * xf, axis=-1, keepdims=True) + NORM_EPS)).astype(x.dtype)

def split_columns(t, widths):
    points, acc = [], 0
    for w in widths[:-1]:
        acc += w
        points.append(acc)
    return jnp.split(t, points, axis=-1)

def causal_short_conv(x, w):
    k_taps, s = w.shape[0], x.shape[1]
    xp = jnp.pad(x, ((0, 0), (k_taps - 1, 0), (0, 0)))
    out = xp[:, 0:s] * w[0]
    for i in range(1, k_taps):
        out = out + xp[:, i:i + s] * w[i]
    return out

def rope_tables(positions):
    inv_freq = ROPE_THETA ** (-jnp.arange(0, MLA_ROPE, 2, dtype=jnp.float32) / MLA_ROPE)
    ang = positions.astype(jnp.float32)[..., None] * inv_freq
    return jnp.cos(ang), jnp.sin(ang)

def apply_rope(x, cos, sin):
    x1, x2 = jnp.split(x, 2, axis=-1)
    cos, sin = cos.astype(x.dtype), sin.astype(x.dtype)
    return jnp.concatenate([x1 * cos - x2 * sin, x1 * sin + x2 * cos], axis=-1)

def gated_delta_rule_chunked(q, k, v, g, beta):
    out_dtype = v.dtype
    b, s, h, dk = q.shape
    dv = v.shape[-1]
    c = GDN_CHUNK
    n = s // c

    def to_chunks(t):
        t = t.astype(jnp.float32).reshape((b, n, c, h) + t.shape[3:])
        return jnp.moveaxis(t, 3, 1)

    q, k, v, g, beta = (to_chunks(t) for t in (q, k, v, g, beta))
    g = jnp.cumsum(g, axis=-1)
    idx = jnp.arange(c)
    causal = idx[:, None] >= idx[None, :]
    strict = idx[:, None] > idx[None, :]
    diff = g[..., :, None] - g[..., None, :]
    decay = jnp.where(causal, jnp.exp(jnp.where(causal, diff, 0.0)), 0.0)

    k_beta = k * beta[..., None]
    a_mat = jnp.where(strict, jnp.einsum('bhnid,bhnjd->bhnij', k_beta, k) * decay, 0.0)
    eye = jnp.eye(c, dtype=jnp.float32)
    t_mat = lax.linalg.triangular_solve(eye + a_mat, jnp.broadcast_to(eye, a_mat.shape),
                                        left_side=True, lower=True)
    u = jnp.einsum('bhnij,bhnjv->bhniv', t_mat, v * beta[..., None])
    w = jnp.einsum('bhnij,bhnjk->bhnik', t_mat, k_beta * jnp.exp(g)[..., None])
    attn = jnp.where(causal, jnp.einsum('bhnik,bhnjk->bhnij', q, k) * decay, 0.0)
    g_last = g[..., -1]
    q_dec = q * jnp.exp(g)[..., None]
    k_dec = k * jnp.exp(g_last[..., None] - g)[..., None]

    xs = tuple(jnp.moveaxis(t, 2, 0) for t in (q_dec, k_dec, u, w, attn, g_last))

    def step(state, inp):
        q_n, k_n, u_n, w_n, a_n, gl_n = inp
        v_new = u_n - jnp.einsum('bhck,bhkv->bhcv', w_n, state)
        o_n = jnp.einsum('bhck,bhkv->bhcv', q_n, state) + jnp.einsum('bhij,bhjv->bhiv', a_n, v_new)
        state = state * jnp.exp(gl_n)[..., None, None] + jnp.einsum('bhck,bhcv->bhkv', k_n, v_new)
        return state, o_n

    state0 = jnp.zeros((b, h, dk, dv), jnp.float32)
    _, o = lax.scan(step, state0, xs)
    o = jnp.transpose(o, (1, 0, 3, 2, 4)).reshape(b, s, h, dv)
    return o.astype(out_dtype)

def causal_block_attention(q, k, v, scale):
    b, s, h, dqk = q.shape
    dv = v.shape[-1]
    nb = s // Q_BLOCK
    q_blocks = jnp.moveaxis(q.reshape(b, nb, Q_BLOCK, h, dqk), 1, 0)
    key_pos = jnp.arange(s)

    def one_block(args):
        q_blk, blk = args
        sc = jnp.einsum('bqhd,bkhd->bhqk', q_blk, k).astype(jnp.float32) * scale
        q_pos = blk * Q_BLOCK + jnp.arange(Q_BLOCK)
        sc = jnp.where(key_pos[None, :] <= q_pos[:, None], sc, -jnp.inf)
        p = jax.nn.softmax(sc, axis=-1).astype(v.dtype)
        return jnp.einsum('bhqk,bkhd->bqhd', p, v)

    out = lax.map(one_block, (q_blocks, jnp.arange(nb)))
    return jnp.moveaxis(out, 0, 1).reshape(b, s, h, dv)

def hybrid_mixer(h, positions, w_in, conv_w, a_log, dt_bias, gdn_norm_w, q_norm_w, w_uq,
                 kv_norm_w, w_ukv, proj_a, proj_b, w_out):
    b, s, _ = h.shape
    proj = h @ w_in
    (qkv_a, z_a, alpha_a, beta_a, c_q, c_kv, k_rope, z_b, gate_a, gate_b) = split_columns(proj, IN_WIDTHS)

    qkv = jax.nn.silu(causal_short_conv(qkv_a, conv_w))
    q_a, k_a, v_a = jnp.split(qkv, [GDN_KEY_W, 2 * GDN_KEY_W], axis=-1)
    q_a = l2_norm(q_a.reshape(b, s, GDN_HEADS, GDN_DK)) * (GDN_DK ** -0.5)
    k_a = l2_norm(k_a.reshape(b, s, GDN_HEADS, GDN_DK))
    v_a = v_a.reshape(b, s, GDN_HEADS, GDN_DV)
    beta = jax.nn.sigmoid(beta_a)
    g_log = -jnp.exp(a_log) * jax.nn.softplus(alpha_a + dt_bias)
    o_a = gated_delta_rule_chunked(q_a, k_a, v_a, g_log, beta)
    o_a = rms_norm(o_a, gdn_norm_w) * jax.nn.silu(z_a.reshape(b, s, GDN_HEADS, GDN_DV))
    y_a = o_a.reshape(b, s, GDN_VAL_W) @ proj_a

    q_b = (rms_norm(c_q, q_norm_w) @ w_uq).reshape(b, s, MLA_HEADS, MLA_QK)
    q_nope, q_rope = jnp.split(q_b, [MLA_NOPE], axis=-1)
    kv = (rms_norm(c_kv, kv_norm_w) @ w_ukv).reshape(b, s, MLA_HEADS, MLA_NOPE + MLA_V)
    k_nope, v_b = jnp.split(kv, [MLA_NOPE], axis=-1)
    cos, sin = rope_tables(positions)
    q_rope = apply_rope(q_rope, cos[:, :, None], sin[:, :, None])
    k_rope = apply_rope(k_rope, cos, sin)
    q_full = jnp.concatenate([q_nope, q_rope], axis=-1)
    k_full = jnp.concatenate(
        [k_nope, jnp.broadcast_to(k_rope[:, :, None], (b, s, MLA_HEADS, MLA_ROPE))], axis=-1)
    o_b = causal_block_attention(q_full, k_full, v_b, 1.0 / math.sqrt(MLA_QK))
    o_b = o_b.reshape(b, s, MLA_VAL_W) * jax.nn.silu(z_b)
    y_b = o_b @ proj_b

    merged = jax.nn.sigmoid(gate_a) * y_a + jax.nn.sigmoid(gate_b) * y_b
    return merged @ w_out

def setup_inputs(seed: int = 0) -> dict:
    key = jax.random.key(seed)
    ks = jax.random.split(key, 18)
    f32 = jnp.float32
    x = jax.random.normal(ks[0], (BATCH, SEQ, D_MODEL), f32)
    offsets = jax.random.randint(ks[1], (BATCH, 1), 0, POS_OFFSET_MAX, dtype=jnp.int32)
    positions = (offsets + jnp.arange(SEQ, dtype=jnp.int32)[None, :]).astype(jnp.int32)
    norm_w = 1.0 + 0.02 * jax.random.normal(ks[2], (DEPTH, D_MODEL), f32)
    w_in = jax.random.normal(ks[3], (DEPTH, D_MODEL, D_IN), f32) * D_MODEL ** -0.5
    conv_w = jax.random.normal(ks[4], (DEPTH, GDN_CONV, GDN_QKV_W), f32) * GDN_CONV ** -0.5
    a_log = jnp.log(jax.random.uniform(ks[5], (DEPTH, GDN_HEADS), f32, 1.0, 16.0))
    dt = jnp.exp(jax.random.uniform(ks[6], (DEPTH, GDN_HEADS), f32, math.log(1e-3), math.log(1e-1)))
    dt_bias = dt + jnp.log(-jnp.expm1(-dt))
    gdn_norm_w = 1.0 + 0.02 * jax.random.normal(ks[7], (DEPTH, GDN_DV), f32)
    q_norm_w = 1.0 + 0.02 * jax.random.normal(ks[8], (DEPTH, MLA_Q_RANK), f32)
    w_uq = jax.random.normal(ks[9], (DEPTH, MLA_Q_RANK, MLA_HEADS * MLA_QK), f32) * MLA_Q_RANK ** -0.5
    kv_norm_w = 1.0 + 0.02 * jax.random.normal(ks[10], (DEPTH, MLA_KV_RANK), f32)
    w_ukv = jax.random.normal(ks[11], (DEPTH, MLA_KV_RANK, MLA_HEADS * (MLA_NOPE + MLA_V)), f32) * MLA_KV_RANK ** -0.5
    proj_a = jax.random.normal(ks[12], (DEPTH, GDN_VAL_W, D_MODEL), f32) * GDN_VAL_W ** -0.5
    proj_b = jax.random.normal(ks[13], (DEPTH, MLA_VAL_W, D_MODEL), f32) * MLA_VAL_W ** -0.5
    w_out = jax.random.normal(ks[14], (DEPTH, D_MODEL, D_MODEL), f32) * D_MODEL ** -0.5
    final_norm_w = 1.0 + 0.02 * jax.random.normal(ks[15], (D_MODEL,), f32)
    return {"x": x, "positions": positions, "norm_w": norm_w, "w_in": w_in, "conv_w": conv_w,
            "a_log": a_log, "dt_bias": dt_bias, "gdn_norm_w": gdn_norm_w, "q_norm_w": q_norm_w,
            "w_uq": w_uq, "kv_norm_w": kv_norm_w, "w_ukv": w_ukv, "proj_a": proj_a,
            "proj_b": proj_b, "w_out": w_out, "final_norm_w": final_norm_w}

def reference(x, positions, norm_w, w_in, conv_w, a_log, dt_bias, gdn_norm_w, q_norm_w, w_uq,
              kv_norm_w, w_ukv, proj_a, proj_b, w_out, final_norm_w):
    for layer in range(DEPTH):
        h = rms_norm(x, norm_w[layer])
        x = x + hybrid_mixer(h, positions, w_in[layer], conv_w[layer], a_log[layer], dt_bias[layer],
                             gdn_norm_w[layer], q_norm_w[layer], w_uq[layer], kv_norm_w[layer],
                             w_ukv[layer], proj_a[layer], proj_b[layer], w_out[layer])
    return rms_norm(x, final_norm_w)


_drawn_inputs = setup_inputs


def setup_inputs(seed=0):
    import zlib

    import numpy as np

    out = dict(_drawn_inputs(seed))
    spreads = {}
    factors = {'norm_w': 5.218,
     'gdn_norm_w': 8.0,
     'q_norm_w': 8.0,
     'kv_norm_w': 8.0,
     'final_norm_w': 2.746}
    for name, (base, spread) in spreads.items():
        noise = np.random.default_rng([zlib.crc32(name.encode()), seed]).standard_normal(out[name].shape)
        drawn = base * np.exp(spread * noise) if base else spread * noise
        out[name] = __import__('jax').numpy.asarray(drawn.astype(out[name].dtype))
    for name, factor in factors.items():
        out[name] = (out[name] * factor).astype(out[name].dtype)
    return out
```

```python
import math
from contextlib import ExitStack

import numpy as np

import concourse.bass as bass
from concourse import mybir

P = 128
D_MODEL, SEQ = 2048, 512
KT = D_MODEL // P
NH = 8
Q_RANK, KV_RANK, ROPE = 512, 256, 64
CQ, CK = Q_RANK // P, KV_RANK // P
NCH = SEQ // P
EPS = 1e-6
SCALE = 1.0 / math.sqrt(128 + ROPE)
TILE = 2048
QT = TILE // 4

T_PRE = 0
N_PRE = CQ + CK + 1
T_QK = T_PRE + N_PRE
T_HEAD = T_QK + 2 * NH
HEAD_TILES = 8
T_MERGE = T_HEAD + HEAD_TILES * NH
T_OUT = T_MERGE + KT
N_TILES = T_OUT + 16

F32, F32R = mybir.dt.float32, mybir.dt.float32r
I32, U8 = mybir.dt.int32, mybir.dt.uint8
ALU, ACT = mybir.AluOpType, mybir.ActivationFunctionType
AX_X = mybir.AxisListType.X

C_IDENT, C_SWAP, C_FOLD, C_ONES, C_MASKQ, C_MASKG = (n * P for n in range(6))
C_FREQ, C_TURN, C_TURN2PI, C_EPS = (6 * P + n for n in range(4))
N_CONST = 6 * P + 4
P_NORM, P_QN, P_KVN, P_GN = 0, KT, KT + CQ, KT + CQ + CK
P_CONV = P_GN + 1
P_DT = P_CONV + 24 * 4
P_ALOG = P_DT + 1
N_PARAM = P_ALOG + 1
NEG = -1e30


class Signal:

    def __init__(self, sem, per_turn, base=0):
        self.sem, self.per_turn, self.base = sem, per_turn, base

    def at(self, i, n):
        return i * self.per_turn + (self.base + n)


def program(nc, xt, x, positions, params, wfinal, stream, consts, masks, out):
    qk_dram = nc.dram_tensor("qk_scratch", [2 * NH, P, SEQ], F32, kind="Internal").ap()
    gb_dram = nc.dram_tensor("gb_scratch", [2 * NH, SEQ], F32, kind="Internal").ap()
    gate_dram = nc.dram_tensor("gate_scratch", [2 * KT, P, SEQ], F32, kind="Internal").ap()
    base_dram = nc.dram_tensor("base_scratch", [64, 16], F32, kind="Internal").ap()
    o_dram = nc.dram_tensor("o_scratch", [2 * NH, P, SEQ], F32, kind="Internal").ap()

    ctx = ExitStack()
    with ctx:
        base = (nc.sbuf_base + 63) // 64 * 64
        at = [base]

        def place(name, shape, dt, size=4, offset=None):
            n = int(np.prod(shape[1:])) * size
            if offset is None:
                offset = at[0]
                at[0] += (n + 63) // 64 * 64
            return nc.alloc_sbuf_tensor_at(name, shape, dt, offset=offset)

        w_raw = [place(f"w_raw{b}", [P, TILE], F32) for b in range(2)]
        w_hi = [place(f"w_hi{b}", [P, TILE], F32R) for b in range(2)]
        w_lo = [place(f"w_lo{b}", [P, TILE], F32R) for b in range(2)]
        const = place("const", [P, N_CONST], F32)
        param = place("param", [P, N_PARAM], F32)
        lmask = place("lmask", [P, 7, P], U8, 1)
        krope = place("krope", [P, SEQ], F32)
        cs = place("cs", [P, SEQ], F32)
        gball = place("gball", [P, NH, 8], F32)
        h_off = at[0]
        h_hi = place("h_hi", [P, KT, SEQ], F32R)
        h_lo = place("h_lo", [P, KT, SEQ], F32R)
        c_off = at[0]
        c_hi = place("c_hi", [P, CQ + CK, SEQ], F32R)
        c_lo = place("c_lo", [P, CQ + CK, SEQ], F32R)
        n_slots = (nc.sbuf_top - at[0] - 64) // (SEQ * 4)
        slots = place("slots", [P, n_slots, SEQ], F32)
        assert n_slots >= 31, n_slots
        m_hi = place("m_hi", [P, KT, SEQ], F32R, offset=c_off)
        m_lo = place("m_lo", [P, KT, SEQ], F32R, offset=c_off + KT * SEQ * 4)
        t_off = c_off + 2 * KT * SEQ * 4
        gate_in = place("gate_in", [P, 2, 2, SEQ], F32, offset=t_off)
        ya = place("ya", [P, SEQ], F32, offset=t_off + 8192)
        yb = place("yb", [P, SEQ], F32, offset=t_off + 10240)
        ym = place("ym", [P, SEQ], F32, offset=t_off + 12288)
        o_in = place("o_in", [P, 4, SEQ], F32, offset=t_off + 8192)
        assert t_off + 8192 + 8192 <= nc.sbuf_top
        y = place("y", [P, NCH, D_MODEL], F32, offset=h_off)
        wf = place("wf", [P, D_MODEL], F32, offset=h_off + NCH * D_MODEL * 4)
        ysq = place("ysq", [P, SEQ], F32, offset=h_off + NCH * D_MODEL * 4 + 8192)
        ssum = place("ssum", [P, NCH, 4], F32, offset=h_off + NCH * D_MODEL * 4 + 8192 + 2048)
        stot = place("stot", [P, NCH, 4], F32, offset=h_off + NCH * D_MODEL * 4 + 8192 + 2112)

        def slot(n):
            return slots[:, n, :]

        def blocks(ap):
            return ap.rearrange("p (c n) -> p c n", c=NCH)

        ident, swap = const[:, C_IDENT:C_IDENT + P], const[:, C_SWAP:C_SWAP + P]
        fold, ones = const[:, C_FOLD:C_FOLD + P], const[:, C_ONES:C_ONES + P]
        mask_q, mask_g = const[:, C_MASKQ:C_MASKQ + P], const[:, C_MASKG:C_MASKG + P]
        eps = const[:, C_EPS:C_EPS + 1]

        xs = [slot(k) for k in range(KT)]
        x_sq, x_ln, x_rs, h_tmp = [slot(16), slot(17)], slot(18), slot(19), [slot(20), slot(21)]
        c_raw = [slot(22 + j) for j in range(6)]
        c_sq = [slot(28), slot(29)]
        mask_i = slots[:, 28:30, :].rearrange("p a n -> p (a n)")[:, 0:7 * P].bitcast(I32)
        special, pos_f, ang, turns = slot(18), slot(0), slot(1), slot(2)
        pos_i = slot(4).bitcast(I32)
        gb = slot(5)
        g_abs, g_sp, g_ex, g_ln = slot(6), slot(7), slot(8), slot(3)
        k_x = slot(9)
        c_ln, c_rs, c_tmp = slot(10), [slot(11), slot(12)], [slot(13), slot(14)]
        cv, cv_e, cv_s, cv_q = ([slot(n), slot(n + 1)] for n in (15, 17, 19, 21))
        cv_ln, cv_rs, cv_o = slot(23), slot(24), [slot(25), slot(29)]
        (qh, kh, g_bc, b_bc, kb, e_mat, e_g, kbe, qd, nat, u_mat, t_mat, w_mat, attn, k_dec,
         v_conv, z_a, z_b, z_e, gate_o0, q_n, q_x, k_n, v_tok, prob0, prob1) = (slot(n) for n in range(26))
        prob, gate_o = [prob0, prob1], [gate_o0, z_e]
        p_t = slots[:, 26:30, :]
        rec = slot(30)
        x_c, v_new, state = rec[:, 0:P], rec[:, P:2 * P], rec[:, 2 * P:3 * P]
        small = rec[:, 3 * P:4 * P]
        hs = small[:, 0:8]
        sc_max, sc_nb, sc_sum, sc_r = (small[:, 8 + 4 * n:12 + 4 * n] for n in range(4))
        a_neg = small[0:NH, 32:33]
        dg, v_e, v_sil, v_beta = e_mat, e_mat, v_conv, v_conv
        o_sq, o_ln, o_rs, o_n, o_a, o_b = w_mat, nat, t_mat, kb, q_n, q_x

        bank = [ctx.enter_context(nc.psum_tensor(f"bank{n}", [P, SEQ], F32)) for n in range(8)]
        dense_b = bank[0:2]
        g0, g1, o_bank, misc, a0, a1 = bank[2:8]

        def sem(name):
            return ctx.enter_context(nc.semaphore(name))

        based = []

        def sig(name, per_turn, base=0):
            s = Signal(sem(name), per_turn, base)
            if base:
                based.append(s)
            return s

        raw_in = [sem(f"raw_in{b}") for b in range(2)]
        hi_done, lo_done = sem("hi_done"), sem("lo_done")
        dense_done = sem("dense_done")

        def tile_of(base_t, per, i, j):
            assert per % 2 == 0
            return (base_t + j) % 2, i * per + (base_t + j)

        def load_tile(sp, base_t, per, i, j):
            b, t = tile_of(base_t, per, i, j)
            sp.wait_ge(lo_done, i * 4 * per + 4 * (base_t + j - 1)) if base_t + j >= 2 else None
            sp.dma_start(w_raw[b][:], stream[t]).then_inc(raw_in[b], 16)

        def split_hi(act, base_t, per, i, j, q):
            b = (base_t + j) % 2
            if q == 0:
                act.wait_ge(raw_in[b], i * 8 * per + 16 * ((base_t + j) // 2 + 1))
            if base_t + j >= 2:
                act.wait_ge(dense_done, i * 4 * per + 4 * (base_t + j - 2) + q + 1)
            sl = slice(q * QT, (q + 1) * QT)
            nc.scalar.copy(w_hi[b][:, sl], w_raw[b][:, sl]).then_inc(hi_done, 1)

        def split_lo(dve, base_t, per, i, j, q):
            b = (base_t + j) % 2
            dve.wait_ge(hi_done, i * 4 * per + 4 * (base_t + j) + q + 1)
            sl = slice(q * QT, (q + 1) * QT)
            nc.vector.tensor_tensor(w_lo[b][:, sl], w_raw[b][:, sl], w_hi[b][:, sl].bitcast(F32),
                                    ALU.subtract).then_inc(lo_done, 1)

        def split_wait(pe, base_t, per, i, j, q):
            pe.wait_ge(lo_done, i * 4 * per + 4 * (base_t + j) + q + 1)

        def three(dst, a_hi, a_lo, b_hi, b_lo, start, stop, mid_inc=None):
            nc.tensor.matmul(dst, a_hi, b_hi, start=start, stop=False)
            nc.tensor.matmul(dst, a_hi, b_lo, start=False, stop=False)
            return nc.tensor.matmul(dst, a_lo, b_hi, start=False, stop=stop)

        def dense(pe, base_t, per, i, j, q):
            b = (base_t + j) % 2
            split_wait(pe, base_t, per, i, j, q)
            for k in range(4 * q, 4 * q + 4):
                sl = slice(k * P, (k + 1) * P)
                mm = three(dense_b[b][:], w_hi[b][:, sl], w_lo[b][:, sl], h_hi[:, k, :], h_lo[:, k, :],
                           k == 0, k == KT - 1)
            mm.then_inc(dense_done, 1)

        def dense_ready(eng, base_t, per, i, j):
            eng.wait_ge(dense_done, i * 4 * per + 4 * (base_t + j) + 4)

        mask_done = sem("mask_done")
        const_in, x_in, pos_in = sem("const_in"), [sem(f"x_in{n}") for n in range(4)], sem("pos_in")
        xsq_done, xsum_done, xrs_done = sem("xsq_done"), sem("xsum_done"), sem("xrs_done")
        hm_done, hh_done, hl_done = sem("hm_done"), sem("hh_done"), sem("hl_done")
        craw_done, csq_done, csum_done, crs_done = sem("craw_done"), sem("csq_done"), sem("csum_done"), sem("crs_done")
        cm_done, ch_done, cl_done = sem("cm_done"), sem("ch_done"), sem("cl_done")
        spec_done, rope_v, cs_done, decay_v, decay_a = (sem(n) for n in ("spec_done", "rope_v", "cs_done", "decay_v", "decay_a"))
        gbt_done, gball_done, gb_stored = sem("gbt_done"), sem("gball_done"), sem("gb_stored")
        swap_done, kx_done, fold_done, krope_done = sem("swap_done"), sem("kx_done"), sem("fold_done"), sem("krope_done")
        conv_done, cve_done, cvs_done, cvq_done = sem("conv_done"), sem("cve_done"), sem("cvs_done"), sem("cvq_done")
        cvsum_done, cvln_done, cvrs_done, cvo_done = sem("cvsum_done"), sem("cvln_done"), sem("cvrs_done"), sem("cvo_done")
        qk_stored = [sig("q_stored", 16, 16), sig("k_stored", 16, 16)]

        head_in = sig("head_in", 64)
        kb_s, hs_s, dg_s, e_s, eg_s, dec_s = sig("kb_s", 1), sig("hs_s", 1), sig("dg_s", 4), sig("e_s", 1), sig("eg_s", 1), sig("dec_s", 2)
        kk_s, ktr_s, qk_s, nat_s, kdec_s, attn_s = (sig(n, 1) for n in ("kk_s", "ktr_s", "qk_s", "nat_s", "kdec_s", "attn_s"))
        u_s, t_s, w_s, wc_s, y_s, tt_s, ttc_s = sig("u_s", 8), sig("t_s", 5), sig("w_s", 6), sig("wc_s", 6), sig("y_s", 6, 1), sig("tt_s", 1), sig("ttc_s", 1)
        vconv_s, vexp_s, vsil_s, vtr_s, vb_s = sig("vconv_s", 4), sig("vexp_s", 1), sig("vsil_s", 1), sig("vtr_s", 1), sig("vb_s", 1)
        ze_s, z_s, gate_s = sig("ze_s", 2), sig("z_s", 2), sig("gate_s", 4, 2)
        gate_st = [sig("gate_st_even", 32, 16), sig("gate_st_odd", 32, 16)]
        qn_p, qx_p, kn_p = (sig(n, 1) for n in ("qn_p", "qx_p", "kn_p"))
        qn_s, qx_s, kn_s, vt_s = (sig(n, 1) for n in ("qn_s", "qx_s", "kn_s", "vt_s"))
        sc_p, msk_s, max_s, nb_s, rc_s, pn_s = (sig(n, 4) for n in ("sc_p", "msk_s", "max_s", "nb_s", "rc_s", "pn_s"))
        ex_s = sig("ex_s", 4, 1)
        pt_p, pt_s = sig("pt_p", 4), sig("pt_s", 4)
        pv_p, ob_s = sig("pv_p", 1, 1), sig("ob_s", 1, 1)
        ks_p, x_s, vn_p, vn_s, up_p, st_s = sig("ks_p", 3), sig("x_s", 3, 1), sig("vn_p", 4), sig("vn_s", 4, 1), sig("up_p", 3), sig("st_s", 3)
        o_p, on_p, oln_s, on_s, oa_s = (sig(n, 1, 1) for n in ("o_p", "on_p", "oln_s", "on_s", "oa_s"))
        osq_s, ors_s = sig("osq_s", 1), sig("ors_s", 1)
        o_st = sig("o_st", 32, 16)
        o_in_s, oh_s, ol_s = [sem(f"o_in_s{n}") for n in range(4)], sem("oh_s"), sem("ol_s")
        gate_ld = [sem("gate_ld0"), sem("gate_ld1")]
        ya_s, ym_s, mh_s, ml_s = [sig("ya_s0", 2, 1), sig("ya_s1", 2, 1)], sig("ym_s", 2, 1), sem("mh_s"), sig("ml_s", 2, 1)
        resid_in, wf_in = sem("resid_in"), sem("wf_in")
        tok_p, y_add, ysq_s = sem("tok_p"), [sig(f"y_add{c}", 1, 1) for c in range(NCH)], sig("ysq_s", 4, 1)
        fin_v, fin_a, yn_s, out_st = sem("fin_v"), sem("fin_a"), sem("yn_s"), sem("out_st")

        block = ctx.enter_context(nc.Block())

        @block.sync
        def _(sp):
            sp.dma_start(const[:], consts).then_inc(const_in, 16)
            sp.dma_start(param[:], params).then_inc(const_in, 16)
            sp.dma_start(mask_i, masks).then_inc(const_in, 16)
            for n in range(4):
                sp.dma_start(slots[:, 4 * n:4 * n + 4, :], xt[:, 4 * n:4 * n + 4, :]).then_inc(x_in[n], 16)
            for t in range(T_QK + 2):
                load_tile(sp, T_PRE, 2, 0, t)
            with sp.Fori(1, NH) as i:
                for j in range(2):
                    load_tile(sp, T_QK, 2, i, j)
            with sp.Fori(0, NH) as i:
                for j in range(HEAD_TILES):
                    load_tile(sp, T_HEAD, HEAD_TILES, i, j)
            with sp.Fori(0, KT // 2) as i:
                for j in range(2):
                    load_tile(sp, T_MERGE, 2, i, j)
            with sp.Fori(0, 4) as i:
                for j in range(4):
                    load_tile(sp, T_OUT, 4, i, j)
            for c in range(NCH):
                sp.wait_ge(yn_s, c + 1)
                sp.dma_start(out[c * P:(c + 1) * P, :], y[:, c, :]).then_inc(out_st, 16)
            sp.wait_ge(out_st, 16 * NCH)

        @block.gpsimd
        def _(pool):
            for n, s in enumerate(based):
                if s.base % 16 == 0:
                    pool.dma_start(base_dram[n:n + 1, :], consts[n:n + 1, 0:16]).then_inc(s.sem, 16)
                else:
                    pool.sem_inc(s.sem, s.base)
            pool.wait_ge(hm_done, KT)
            pool.dma_start(pos_i, positions.to_broadcast([P, SEQ])).then_inc(pos_in, 16)
            pool.wait_ge(decay_v, 11)
            pool.dma_start(gb_dram[0:NH, :], gb[0:NH, :]).then_inc(gb_stored, 16)
            pool.dma_start(gb_dram[NH:2 * NH, :], gb[32:32 + NH, :]).then_inc(gb_stored, 16)
            with pool.Fori(0, NH) as i:
                for j in range(2):
                    pool.wait_ge(cvo_done, i * 2 + (j + 1))
                    pool.dma_start(qk_dram[i * 2 + j], cv_o[j]).then_inc(qk_stored[j].sem, 16)
            pool.wait_ge(gb_stored, 32)
            for j in range(2):
                pool.wait_ge(qk_stored[j].sem, qk_stored[j].at(NH - 1, 16))

            def load_head(i):
                pool.dma_start(qh, qk_dram[i * 2]).then_inc(head_in.sem, 16)
                pool.dma_start(kh, qk_dram[i * 2 + 1]).then_inc(head_in.sem, 16)
                pool.dma_start(g_bc, gb_dram[bass.ds(i, 1), :].to_broadcast([P, SEQ])).then_inc(head_in.sem, 16)
                pool.dma_start(b_bc, gb_dram[bass.ds(i + NH, 1), :].to_broadcast([P, SEQ])).then_inc(head_in.sem, 16)

            pool.wait_ge(cl_done, CQ + CK)
            pool.wait_ge(krope_done, 1)
            pool.wait_ge(gball_done, 2)
            pool.wait_ge(cs_done, 1)
            load_head(0)

            def head_stores(i):
                pool.wait_ge(ob_s.sem, ob_s.at(i, 1))
                pool.dma_start(o_dram[i + NH], o_b).then_inc(o_st.sem, 16)
                for n in range(4):
                    pool.wait_ge(gate_s.sem, gate_s.at(i, n + 1))
                    pool.dma_start(gate_dram[i * 4 + n], gate_o[n % 2]).then_inc(gate_st[n % 2].sem, 16)

            with pool.Fori(0, NH - 1) as i:
                pool.wait_ge(qk_s.sem, qk_s.at(i, 1))
                pool.wait_ge(ktr_s.sem, ktr_s.at(i, 1))
                pool.wait_ge(dec_s.sem, dec_s.at(i, 2))
                load_head(i + 1)
                head_stores(i)
                pool.wait_ge(oa_s.sem, oa_s.at(i, 1))
                pool.dma_start(o_dram[i], o_a).then_inc(o_st.sem, 16)
            head_stores(NH - 1)
            pool.wait_ge(oa_s.sem, oa_s.at(NH - 1, 1))
            pool.dma_start(o_dram[NH - 1], o_a).then_inc(o_st.sem, 16)

            pool.wait_ge(o_st.sem, o_st.at(NH - 1, 32))
            for p in range(2):
                pool.wait_ge(gate_st[p].sem, gate_st[p].at(NH - 1, 32))
            for n in range(2 * NH):
                if n >= 4:
                    pool.wait_ge(ol_s, n - 3)
                pool.dma_start(o_in[:, n % 4, :], o_dram[n]).then_inc(o_in_s[n % 4], 16)

            def load_gates(f, p):
                pool.dma_start(gate_in[:, p, 0, :], gate_dram[f]).then_inc(gate_ld[p], 16)
                pool.dma_start(gate_in[:, p, 1, :], gate_dram[f + KT]).then_inc(gate_ld[p], 16)

            load_gates(0, 0)
            load_gates(1, 1)
            with pool.Fori(0, KT // 2 - 1) as i:
                for p in range(2):
                    pool.wait_ge(ya_s[p].sem, ya_s[p].at(i, 2))
                    load_gates(i * 2 + (2 + p), p)
            pool.wait_ge(dense_done, 4 * T_OUT)
            pool.dma_start(y[:], x.rearrange("(c p) d -> p c d", p=P)).then_inc(resid_in, 16)
            pool.dma_start(wf[:], wfinal.to_broadcast([P, D_MODEL])).then_inc(wf_in, 16)

        @block.scalar
        def _(act):
            act.wait_ge(const_in, 48)
            for k in range(KT):
                if k % 4 == 0:
                    act.wait_ge(x_in[k // 4], 16)
                if k >= 2:
                    act.wait_ge(xsum_done, k - 1)
                nc.scalar.activation(x_sq[k % 2], xs[k], ACT.Square).then_inc(xsq_done, 1)
            for q in range(4):
                split_hi(act, 0, 2, 0, 0, q)
            act.wait_ge(xsum_done, KT)
            nc.scalar.activation(x_ln, misc[:], ACT.Ln, bias=eps, scale=1.0 / D_MODEL).then_inc(xrs_done, 1)
            act.wait_ge(xrs_done, 1)
            nc.scalar.activation(x_rs, x_ln, ACT.Exp, scale=-0.5).then_inc(xrs_done, 1)
            for k in range(KT):
                act.wait_ge(hm_done, k + 1)
                nc.scalar.copy(h_hi[:, k, :], h_tmp[k % 2]).then_inc(hh_done, 1)

            for t in range(CQ + CK):
                for q in range(4):
                    split_hi(act, 0, 2, 0, t + 1, q)
                dense_ready(act, 0, 2, 0, t)
                nc.scalar.copy(c_raw[t], dense_b[t % 2][:]).then_inc(craw_done, 1)
                act.wait_ge(mask_done, 1)
                if t >= 2:
                    act.wait_ge(csum_done, t - 1)
                nc.scalar.activation(c_sq[t % 2], dense_b[t % 2][:], ACT.Square).then_inc(csq_done, 1)
            for q in range(4):
                split_hi(act, 0, 2, 0, N_PRE, q)
            for n, (bank_c, width, count) in enumerate(((misc, Q_RANK, CQ), (o_bank, KV_RANK, CQ + CK))):
                act.wait_ge(csum_done, count)
                if n:
                    act.wait_ge(crs_done, 2)
                nc.scalar.activation(c_ln, bank_c[:], ACT.Ln, bias=eps, scale=1.0 / width).then_inc(crs_done, 1)
                act.wait_ge(crs_done, 2 * n + 1)
                nc.scalar.activation(c_rs[n], c_ln, ACT.Exp, scale=-0.5).then_inc(crs_done, 1)
            for j in range(CQ + CK):
                act.wait_ge(cm_done, j + 1)
                nc.scalar.copy(c_hi[:, j, :], c_tmp[j % 2]).then_inc(ch_done, 1)
            dense_ready(act, 0, 2, 0, N_PRE - 1)
            nc.scalar.copy(special, dense_b[(N_PRE - 1) % 2][:]).then_inc(spec_done, 1)
            act.wait_ge(decay_v, 2)
            nc.scalar.activation(g_ex[0:NH, :], g_abs[0:NH, :], ACT.Exp, scale=-1.0).then_inc(decay_a, 1)
            act.wait_ge(decay_a, 1)
            nc.scalar.activation(g_ln[0:NH, :], g_ex[0:NH, :], ACT.Ln, bias=ones[0:NH, 0:1]).then_inc(decay_a, 1)
            nc.scalar.activation(g_ex[32:32 + NH, :], special[32:32 + NH, :], ACT.Tanh, scale=0.5).then_inc(decay_a, 1)
            nc.scalar.activation(a_neg, param[0:NH, P_ALOG:P_ALOG + 1], ACT.Exp).then_inc(decay_a, 1)
            act.wait_ge(rope_v, 8)
            nc.scalar.activation(cs[:], ang, ACT.Sin).then_inc(cs_done, 1)

            def silu_tanh(i, j):
                act.wait_ge(conv_done, i * 8 + 4 * j + 4)
                nc.scalar.activation(cv_e[j], cv[j], ACT.Tanh, scale=0.5).then_inc(cve_done, 1)

            def square(i, j):
                act.wait_ge(cvs_done, i * 2 + (j + 1))
                nc.scalar.activation(cv_q[j], cv_s[j], ACT.Square).then_inc(cvq_done, 1)

            def norm_factor(n, j):
                act.wait_ge(cvsum_done, n + 1)
                if not (isinstance(n, int) and n == 0):
                    act.wait_ge(cvo_done, n)
                nc.scalar.activation(cv_ln, misc[:], ACT.Ln, bias=eps, scale=0.25).then_inc(cvln_done, 1)
                act.wait_ge(cvln_done, n + 1)
                nc.scalar.activation(cv_rs, cv_ln, ACT.Exp, scale=-0.5).then_inc(cvrs_done, 1)

            def qk_turn(i, first):
                for j in range(2):
                    for q in range(4):
                        split_hi(act, T_QK, 2, i, j + 1, q)
                        if q == 1 and not (first and j == 0):
                            norm_factor(i * 2 + (j - 1), 1 - j)
                    silu_tanh(i, j)
                    square(i, j)

            qk_turn(0, True)
            with act.Fori(1, NH) as i:
                qk_turn(i, False)
            norm_factor(2 * NH - 1, 1)

            with act.Fori(0, NH) as i:
                def hi(j, *qs):
                    for q in qs:
                        split_hi(act, T_HEAD, HEAD_TILES, i, j, q)

                def w_copy(l):
                    act.wait_ge(w_s.sem, w_s.at(i, l))
                    act.wait_ge(y_s.sem, y_s.at(i, l - 1))
                    nc.scalar.copy(w_mat, g1[:]).then_inc(wc_s.sem, 1)

                def exp_scores(b):
                    n = (b + 1) * P
                    src = a0 if b % 2 == 0 else a1
                    act.wait_ge(nb_s.sem, nb_s.at(i, b + 1))
                    if b >= 2:
                        act.wait_ge(pt_p.sem, pt_p.at(i, b - 1))
                    nc.scalar.activation(prob[b % 2][:, 0:n], src[:, 0:n], ACT.Exp, bias=sc_nb[:, b:b + 1],
                                         scale=SCALE, accum_out=sc_sum[:, b:b + 1]).then_inc(ex_s.sem, 1)

                def pt_copy(b):
                    act.wait_ge(pt_p.sem, pt_p.at(i, b + 1))
                    if b == 0:
                        act.wait_ge(pv_p.sem, pv_p.at(i, 0))
                    nc.scalar.copy(p_t[:, 0:b + 1, b * P:(b + 1) * P], blocks(misc[:])[:, 0:b + 1, :])\
                        .then_inc(pt_s.sem, 1)

                def z_tanh(n, j):
                    dense_ready(act, T_HEAD, HEAD_TILES, i, j)
                    if n == 0:
                        act.wait_ge(gate_st[1].sem, gate_st[1].at(i, 0))
                    else:
                        act.wait_ge(z_s.sem, z_s.at(i, 1))
                    nc.scalar.activation(z_e, dense_b[(T_HEAD + j) % 2][:], ACT.Tanh, scale=0.5).then_inc(ze_s.sem, 1)

                def gate_tanh(n):
                    dense_ready(act, T_HEAD, HEAD_TILES, i, 4 + n)
                    act.wait_ge(gate_st[n % 2].sem, gate_st[n % 2].at(i, 16 * (n // 2)))
                    if n == 1:
                        act.wait_ge(z_s.sem, z_s.at(i, 2))
                    nc.scalar.activation(gate_o[n % 2], dense_b[(T_HEAD + n) % 2][:], ACT.Tanh, scale=0.5)\
                        .then_inc(gate_s.sem, 1)

                def vn_copy(c):
                    act.wait_ge(vn_p.sem, vn_p.at(i, c + 1))
                    if c:
                        act.wait_ge(up_p.sem, up_p.at(i, c))
                    nc.scalar.copy(v_new, g0[:, 0:P]).then_inc(vn_s.sem, 1)

                act.wait_ge(dg_s.sem, dg_s.at(i, 4))
                nc.scalar.activation(e_mat, dg, ACT.Exp).then_inc(e_s.sem, 1)
                nc.scalar.activation(e_g, g_bc, ACT.Exp).then_inc(eg_s.sem, 1)
                hi(1, 0, 1, 2)
                act.wait_ge(on_p.sem, on_p.at(i, 0))
                w_copy(1)
                hi(1, 3)
                hi(2, 0)
                act.wait_ge(qn_p.sem, qn_p.at(i, 1))
                act.wait_ge(o_st.sem, o_st.at(i, 0))
                nc.scalar.copy(q_n, a0[:]).then_inc(qn_s.sem, 1)
                act.wait_ge(vconv_s.sem, vconv_s.at(i, 4))
                nc.scalar.activation(v_e, v_conv, ACT.Tanh, scale=0.5).then_inc(vexp_s.sem, 1)
                w_copy(2)
                hi(2, 1)
                act.wait_ge(kn_p.sem, kn_p.at(i, 1))
                nc.scalar.copy(k_n, a0[:]).then_inc(kn_s.sem, 1)
                hi(2, 2)
                dense_ready(act, T_HEAD, HEAD_TILES, i, 1)
                nc.scalar.copy(v_tok, a1[:]).then_inc(vt_s.sem, 1)
                hi(2, 3)
                hi(3, 0)
                w_copy(3)
                hi(3, 1, 2)
                exp_scores(0)
                w_copy(4)
                hi(3, 3)
                exp_scores(1)
                z_tanh(0, 2)
                hi(4, 0)
                w_copy(5)
                pt_copy(0)
                hi(4, 1)
                exp_scores(2)
                pt_copy(1)
                hi(4, 2)
                exp_scores(3)
                hi(4, 3)
                act.wait_ge(tt_s.sem, tt_s.at(i, 1))
                nc.scalar.copy(t_mat, g1[:]).then_inc(ttc_s.sem, 1)
                z_tanh(1, 3)
                w_copy(6)
                pt_copy(2)
                hi(5, 0)
                pt_copy(3)
                hi(5, 1)
                vn_copy(0)
                hi(5, 2, 3)
                gate_tanh(0)
                hi(6, 0)
                vn_copy(1)
                hi(6, 1, 2, 3)
                gate_tanh(1)
                vn_copy(2)
                hi(7, 0, 1, 2, 3)
                vn_copy(3)
                gate_tanh(2)
                hi(8, 0)
                act.wait_ge(o_p.sem, o_p.at(i, 1))
                nc.scalar.activation(o_sq, o_bank[:], ACT.Square).then_inc(osq_s.sem, 1)
                hi(8, 1)
                act.wait_ge(on_p.sem, on_p.at(i, 1))
                nc.scalar.activation(o_ln, misc[:], ACT.Ln, bias=eps, scale=1.0 / P).then_inc(oln_s.sem, 1)
                act.wait_ge(oln_s.sem, oln_s.at(i, 1))
                nc.scalar.activation(o_rs, o_ln, ACT.Exp, scale=-0.5).then_inc(ors_s.sem, 1)
                hi(8, 2, 3)
                gate_tanh(3)

            for n in range(2 * NH):
                act.wait_ge(o_in_s[n % 4], 16 * (n // 4 + 1))
                act.wait_ge(dense_done, 4 * (T_MERGE - 1) + n // 4 + 1)
                nc.scalar.copy(h_hi[:, n, :], o_in[:, n % 4, :]).then_inc(oh_s, 1)

            with act.Fori(0, KT // 2) as i:
                for j in range(2):
                    for q in range(4):
                        split_hi(act, T_MERGE, 2, i, j + 1, q)
                    act.wait_ge(ym_s.sem, ym_s.at(i, j + 1))
                    nc.scalar.copy(m_hi[:, bass.ds(i * 2 + j, 1), :], ym[:].unsqueeze(1)).then_inc(mh_s, 1)

            def out_turn(i, last):
                for j in range(4):
                    if not (last and j == 3):
                        for q in range(4):
                            split_hi(act, T_OUT, 4, i, j + 1, q)
                for c in range(NCH):
                    act.wait_ge(y_add[c].sem, y_add[c].at(i, 1))
                    act.wait_ge(ysq_s.sem, ysq_s.at(i, c))
                    nc.scalar.activation(ysq[:], y[:, c, bass.ds(i * SEQ, SEQ)], ACT.Square,
                                         accum_out=ssum[:, c, bass.ds(i, 1)]).then_inc(ysq_s.sem, 1)

            with act.Fori(0, 3) as i:
                out_turn(i, False)
            out_turn(3, True)
            act.wait_ge(fin_v, NCH)
            nc.scalar.activation(stot[:, :, 1], stot[:, :, 0], ACT.Ln, bias=eps, scale=1.0 / D_MODEL).then_inc(fin_a, 1)
            act.wait_ge(fin_a, 1)
            nc.scalar.activation(stot[:, :, 2], stot[:, :, 1], ACT.Exp, scale=-0.5).then_inc(fin_a, 1)

        @block.vector
        def _(dve):
            dve.wait_ge(const_in, 48)
            nc.vector.tensor_copy(lmask[:].rearrange("p a n -> p (a n)"), mask_i).then_inc(mask_done, 1)
            for q in range(4):
                split_lo(dve, 0, 2, 0, 0, q)

            def h_scaled(k):
                if k == 0:
                    dve.wait_ge(xrs_done, 2)
                if k >= 2:
                    dve.wait_ge(hl_done, k - 1)
                nc.vector.scalar_tensor_tensor(h_tmp[k % 2], xs[k], param[:, P_NORM + k:P_NORM + k + 1], x_rs,
                                               ALU.mult, ALU.mult).then_inc(hm_done, 1)

            def h_low(k):
                dve.wait_ge(hh_done, k + 1)
                nc.vector.tensor_tensor(h_lo[:, k, :], h_tmp[k % 2], h_hi[:, k, :].bitcast(F32),
                                        ALU.subtract).then_inc(hl_done, 1)

            for k in range(KT):
                h_scaled(k)
                if k >= 1:
                    h_low(k - 1)
            h_low(KT - 1)

            dve.wait_ge(pos_in, 16)
            c1, c2, magic = 6.28125, float(np.float32(2 * math.pi - 6.28125)), 1.5 * 2.0 ** 23
            nc.vector.tensor_copy(pos_f, pos_i).then_inc(rope_v, 1)
            dve.wait_ge(rope_v, 1)
            nc.vector.tensor_scalar(ang, pos_f, const[:, C_FREQ:C_FREQ + 1], None, ALU.mult).then_inc(rope_v, 1)
            dve.wait_ge(rope_v, 2)
            nc.vector.tensor_scalar(turns, ang, 1.0 / (2 * math.pi), const[:, C_TURN:C_TURN + 1],
                                    ALU.mult, ALU.add).then_inc(rope_v, 1)
            dve.wait_ge(rope_v, 3)
            nc.vector.tensor_scalar(turns, turns, magic, -magic, ALU.add, ALU.add).then_inc(rope_v, 1)
            dve.wait_ge(rope_v, 4)
            nc.vector.scalar_tensor_tensor(ang, turns, -c1, ang, ALU.mult, ALU.add).then_inc(rope_v, 1)
            for q in range(4):
                split_lo(dve, 0, 2, 0, 1, q)
            dve.wait_ge(rope_v, 5)
            nc.vector.scalar_tensor_tensor(ang, turns, -c2, ang, ALU.mult, ALU.add).then_inc(rope_v, 1)
            dve.wait_ge(rope_v, 6)
            nc.vector.tensor_scalar(ang, ang, const[:, C_TURN2PI:C_TURN2PI + 1], 3.141592, ALU.add, ALU.min)\
                .then_inc(rope_v, 1)
            dve.wait_ge(rope_v, 7)
            nc.vector.tensor_scalar(ang, ang, -3.141592, None, ALU.max).then_inc(rope_v, 1)
            for t in range(2, N_PRE + 1):
                for q in range(4):
                    split_lo(dve, 0, 2, 0, t, q)

            def c_scaled(j):
                n = 0 if j < CQ else 1
                dve.wait_ge(crs_done, 2 * n + 2)
                if j >= 2:
                    dve.wait_ge(cl_done, j - 1)
                nc.vector.scalar_tensor_tensor(c_tmp[j % 2], c_raw[j], param[:, P_QN + j:P_QN + j + 1], c_rs[n],
                                               ALU.mult, ALU.mult).then_inc(cm_done, 1)

            def c_low(j):
                dve.wait_ge(ch_done, j + 1)
                nc.vector.tensor_tensor(c_lo[:, j, :], c_tmp[j % 2], c_hi[:, j, :].bitcast(F32),
                                        ALU.subtract).then_inc(cl_done, 1)

            for j in range(CQ + CK):
                c_scaled(j)
                if j >= 1:
                    c_low(j - 1)
            c_low(CQ + CK - 1)

            heads, brows = slice(0, NH), slice(32, 32 + NH)
            dt_bias = param[heads, P_DT:P_DT + 1]
            dve.wait_ge(spec_done, 1)
            nc.vector.tensor_scalar(g_sp[heads, :], special[heads, :], dt_bias, None, ALU.add).then_inc(decay_v, 1)
            dve.wait_ge(decay_v, 1)
            nc.vector.scalar_tensor_tensor(g_abs[heads, :], g_sp[heads, :], -1.0, g_sp[heads, :], ALU.mult, ALU.max)\
                .then_inc(decay_v, 1)
            nc.vector.tensor_scalar(g_sp[heads, :], g_sp[heads, :], 0.0, None, ALU.max).then_inc(decay_v, 1)
            dve.wait_ge(decay_v, 3)
            dve.wait_ge(decay_a, 4)
            nc.vector.tensor_tensor(g_sp[heads, :], g_sp[heads, :], g_ln[heads, :], ALU.add).then_inc(decay_v, 1)
            dve.wait_ge(decay_v, 4)
            nc.vector.tensor_scalar(g_sp[heads, :], g_sp[heads, :], a_neg, -1.0, ALU.mult, ALU.mult).then_inc(decay_v, 1)
            nc.vector.memset(gb, 0.0).then_inc(decay_v, 1)
            dve.wait_ge(decay_v, 6)
            for c in range(NCH):
                sl = slice(c * P, (c + 1) * P)
                nc.vector.tensor_tensor_scan(gb[heads, sl], ones[heads, 0:P], g_sp[heads, sl], 0.0,
                                             ALU.mult, ALU.add).then_inc(decay_v, 1)
            nc.vector.tensor_scalar(gb[brows, :], g_ex[brows, :], 0.5, 0.5, ALU.mult, ALU.add).then_inc(decay_v, 1)

            def conv(src, dst, wcol, done, i_wait, n0):
                def tap(k):
                    return param[:, bass.ds(wcol + k, 1)] if not isinstance(wcol, int) else param[:, wcol + k:wcol + k + 1]
                nc.vector.tensor_scalar(dst, src[:], tap(3), None, ALU.mult).then_inc(done, 1)
                for s in range(1, 4):
                    dve.wait_ge(done, i_wait(n0 + s))
                    ins = nc.vector.scalar_tensor_tensor(dst[:, s:SEQ], src[:, 0:SEQ - s], tap(3 - s), dst[:, s:SEQ],
                                                         ALU.mult, ALU.add)
                    ins.then_inc(done, 1)

            def qk_conv(i, j):
                dense_ready(dve, T_QK, 2, i, j)
                b = (T_QK + j) % 2
                if not (isinstance(i, int) and i == 0):
                    dve.wait_ge(cve_done, i * 2 + (j - 1)) if j else dve.wait_ge(cve_done, i * 2 - 1)
                conv(dense_b[b], cv[j], i * 4 + (P_CONV + 32 * j), conv_done, lambda n: i * 8 + n, 4 * j)
                dve.wait_ge(cve_done, i * 2 + (j + 1))
                if not (isinstance(i, int) and i == 0):
                    dve.wait_ge(cvo_done, i * 2 + (j - 1))
                nc.vector.scalar_tensor_tensor(cv_s[j], cv_e[j], 1.0, cv[j], ALU.add, ALU.mult).then_inc(cvs_done, 1)

            def qk_norm(n, j, turn):
                dve.wait_ge(cvrs_done, n + 1)
                if turn is not None:
                    dve.wait_ge(qk_stored[j].sem, qk_stored[j].at(turn, 0))
                nc.vector.scalar_tensor_tensor(cv_o[j], cv_s[j], 0.5 * float(P) ** -0.5 if j == 0 else 0.5, cv_rs,
                                               ALU.mult, ALU.mult).then_inc(cvo_done, 1)

            def rope_key():
                dve.wait_ge(swap_done, 1)
                dve.wait_ge(cs_done, 1)
                nc.vector.tensor_tensor(k_x, misc[:], cs[:], ALU.mult).then_inc(kx_done, 1)
                dve.wait_ge(gbt_done, 1)
                gt = o_bank[:].rearrange("p (c n) -> p n c", c=NCH)
                nc.vector.tensor_scalar(gball[:, :, 0:4], gt[:, 0:NH, :], -1.0, None, ALU.mult).then_inc(gball_done, 1)
                nc.vector.tensor_scalar(gball[:, :, 4:8], gt[:, 32:32 + NH, :], 0.5, None, ALU.mult).then_inc(gball_done, 1)
                dve.wait_ge(fold_done, 1)
                nc.vector.tensor_copy(krope[:], a0[:]).then_inc(krope_done, 1)

            for q in range(4):
                split_lo(dve, T_QK, 2, 0, 1, q)
            rope_key()
            qk_conv(0, 0)
            for q in range(4):
                split_lo(dve, T_QK, 2, 0, 2, q)
            qk_norm(0, 0, None)
            qk_conv(0, 1)
            with dve.Fori(1, NH) as i:
                for j in range(2):
                    for q in range(4):
                        split_lo(dve, T_QK, 2, i, j + 1, q)
                    qk_norm(i * 2 + (j - 1), 1 - j, i if j else i - 1)
                    qk_conv(i, j)
            qk_norm(2 * NH - 1, 1, NH - 1)

            with dve.Fori(0, NH) as i:
                def lo(j, *qs):
                    for q in qs:
                        split_lo(dve, T_HEAD, HEAD_TILES, i, j, q)

                def w(s, n):
                    dve.wait_ge(s.sem, s.at(i, n))

                waiter = small[:, 40:41]

                def update(l):
                    w(y_s, l)
                    nc.vector.memset(waiter, 0.0)
                    nc.vector.copy_predicated(blocks(u_mat), lmask[:, l:l + 1, :].to_broadcast([P, NCH, P]),
                                              blocks(g0[:])).then_inc(u_s.sem, 1)
                    if l <= 4:
                        w(u_s, l + 2)
                        nc.vector.transpose(t_mat, u_mat).then_inc(t_s.sem, 1)

                def score_max(b):
                    n = (b + 1) * P
                    src = a0 if b % 2 == 0 else a1
                    w(sc_p, b + 1)
                    nc.vector.tensor_tensor(src[:, b * P:n], src[:, b * P:n], mask_q, ALU.add).then_inc(msk_s.sem, 1)
                    w(msk_s, b + 1)
                    nc.vector.reduce_max(sc_max[:, b:b + 1], src[:, 0:n], AX_X).then_inc(max_s.sem, 1)
                    w(max_s, b + 1)
                    nc.vector.tensor_scalar(sc_nb[:, b:b + 1], sc_max[:, b:b + 1], -SCALE, None, ALU.mult)\
                        .then_inc(nb_s.sem, 1)

                def normalise(b):
                    n = (b + 1) * P
                    w(ex_s, b + 1)
                    nc.vector.reciprocal(sc_r[:, b:b + 1], sc_sum[:, b:b + 1]).then_inc(rc_s.sem, 1)
                    w(rc_s, b + 1)
                    nc.vector.tensor_scalar(prob[b % 2][:, 0:n], prob[b % 2][:, 0:n], sc_r[:, b:b + 1], None, ALU.mult)\
                        .then_inc(pn_s.sem, 1)

                def z_silu(n, dst):
                    w(ze_s, n + 1)
                    nc.vector.scalar_tensor_tensor(dst, z_e, 1.0, dense_b[(T_HEAD + 2 + n) % 2][:], ALU.add, ALU.mult)\
                        .then_inc(z_s.sem, 1)

                def x_chunk(c):
                    w(ks_p, c)
                    if c >= 1:
                        w(vn_p, c)
                    nc.vector.tensor_tensor(x_c, v_beta[:, c * P:(c + 1) * P], g1[:, 0:P], ALU.subtract)\
                        .then_inc(x_s.sem, 1)

                def state_update(c):
                    w(up_p, c + 1)
                    if c == 0:
                        ins = nc.vector.tensor_copy(state, g1[:, 0:P])
                    else:
                        w(st_s, c)
                        ins = nc.vector.scalar_tensor_tensor(state, state, e_g[:, (c + 1) * P - 1:(c + 1) * P], g1[:, 0:P],
                                                             ALU.mult, ALU.add)
                    ins.then_inc(st_s.sem, 1)

                w(head_in, 64)
                w(o_p, 0)
                nc.vector.tensor_copy(hs, gball[:, bass.ds(i, 1), :].rearrange("p a n -> p (a n)")).then_inc(hs_s.sem, 1)
                w(hs_s, 1)
                for c in range(NCH):
                    sl = slice(c * P, (c + 1) * P)
                    nc.vector.scalar_tensor_tensor(dg[:, sl], g_bc[:, sl], hs[:, c:c + 1], mask_g, ALU.add, ALU.add)\
                        .then_inc(dg_s.sem, 1)
                w(oa_s, 0)
                nc.vector.tensor_tensor(kb, kh, b_bc, ALU.mult).then_inc(kb_s.sem, 1)
                w(kb_s, 1)
                w(eg_s, 1)
                nc.vector.tensor_tensor(kbe, kb, e_g, ALU.mult).then_inc(dec_s.sem, 1)
                nc.vector.tensor_tensor(qd, qh, e_g, ALU.mult).then_inc(dec_s.sem, 1)
                w(kk_s, 1)
                w(e_s, 1)
                nc.vector.scalar_tensor_tensor(nat, g0[:], -1.0, e_mat, ALU.mult, ALU.mult).then_inc(nat_s.sem, 1)
                nc.vector.tensor_copy(blocks(u_mat), ident.unsqueeze(1).to_broadcast([P, NCH, P])).then_inc(u_s.sem, 1)
                w(u_s, 1)
                w(nat_s, 1)
                nc.vector.memset(waiter, 0.0)
                nc.vector.copy_predicated(blocks(u_mat), lmask[:, 0:1, :].to_broadcast([P, NCH, P]),
                                          blocks(nat)).then_inc(u_s.sem, 1)
                w(u_s, 2)
                nc.vector.transpose(t_mat, u_mat).then_inc(t_s.sem, 1)
                w(ktr_s, 1)
                nc.vector.tensor_tensor(blocks(k_dec), blocks(misc[:]), blocks(e_mat)[:, :, P - 1:P].to_broadcast([P, NCH, P]),
                                        ALU.mult).then_inc(kdec_s.sem, 1)
                lo(1, 0, 1)
                w(qk_s, 1)
                nc.vector.tensor_tensor(attn, g0[:], e_mat, ALU.mult).then_inc(attn_s.sem, 1)
                lo(1, 2, 3)
                update(1)
                dense_ready(dve, T_HEAD, HEAD_TILES, i, 0)
                conv(dense_b[T_HEAD % 2], v_conv, i * 4 + (P_CONV + 64), vconv_s.sem, lambda n: vconv_s.at(i, n), 0)
                w(qx_p, 1)
                w(o_st, 0)
                nc.vector.tensor_tensor(q_x, a1[:], cs[:], ALU.mult).then_inc(qx_s.sem, 1)
                lo(2, 0)
                update(2)
                w(vexp_s, 1)
                nc.vector.scalar_tensor_tensor(v_sil, v_e, 1.0, v_conv, ALU.add, ALU.mult).then_inc(vsil_s.sem, 1)
                lo(2, 1, 2, 3)
                lo(3, 0)
                update(3)
                w(vtr_s, 1)
                nc.vector.tensor_tensor(blocks(v_beta), blocks(misc[:]), hs[:, 4:8].unsqueeze(2).to_broadcast([P, NCH, P]),
                                        ALU.mult).then_inc(vb_s.sem, 1)
                lo(3, 1)
                score_max(0)
                lo(3, 2)
                normalise(0)
                score_max(1)
                lo(3, 3)
                update(4)
                z_silu(0, z_b)
                lo(4, 0)
                normalise(1)
                update(5)
                score_max(2)
                lo(4, 1)
                score_max(3)
                normalise(2)
                lo(4, 2)
                normalise(3)
                lo(4, 3)
                z_silu(1, z_a)
                update(6)
                lo(5, 0, 1)
                state_update(0)
                lo(5, 2)
                x_chunk(1)
                w(pv_p, 1)
                nc.vector.scalar_tensor_tensor(o_b, a0[:], 0.5, z_b, ALU.mult, ALU.mult).then_inc(ob_s.sem, 1)
                lo(5, 3)
                lo(6, 0)
                state_update(1)
                lo(6, 1)
                x_chunk(2)
                lo(6, 2, 3)
                state_update(2)
                lo(7, 0)
                x_chunk(3)
                lo(7, 1, 2, 3)
                lo(8, 0, 1)
                w(ors_s, 1)
                nc.vector.scalar_tensor_tensor(o_n, o_bank[:], param[:, P_GN:P_GN + 1], o_rs, ALU.mult, ALU.mult)\
                    .then_inc(on_s.sem, 1)
                w(on_s, 1)
                nc.vector.scalar_tensor_tensor(o_a, o_n, 0.5, z_a, ALU.mult, ALU.mult).then_inc(oa_s.sem, 1)
                lo(8, 2, 3)

            for n in range(2 * NH):
                dve.wait_ge(oh_s, n + 1)
                nc.vector.tensor_tensor(h_lo[:, n, :], o_in[:, n % 4, :], h_hi[:, n, :].bitcast(F32), ALU.subtract)\
                    .then_inc(ol_s, 1)
            dve.wait_ge(ol_s, 2 * NH)

            with dve.Fori(0, KT // 2) as i:
                for j in range(2):
                    for q in range(4):
                        split_lo(dve, T_MERGE, 2, i, j + 1, q)
                    b = (T_MERGE + j) % 2
                    dense_ready(dve, T_MERGE, 2, i, j)
                    dve.wait_ge(gate_ld[j], i * 32 + 32)
                    dve.wait_ge(ym_s.sem, ym_s.at(i, j))
                    nc.vector.scalar_tensor_tensor(ya[:], gate_in[:, j, 0, :], 1.0, dense_b[b][:], ALU.add, ALU.mult).then_inc(ya_s[j].sem, 1)
                    nc.vector.scalar_tensor_tensor(yb[:], gate_in[:, j, 1, :], 1.0, (a0, a1)[b][:], ALU.add, ALU.mult).then_inc(ya_s[j].sem, 1)
                    dve.wait_ge(ya_s[j].sem, ya_s[j].at(i, 2))
                    dve.wait_ge(ml_s.sem, ml_s.at(i, j))
                    nc.vector.tensor_tensor(ym[:], ya[:], yb[:], ALU.add).then_inc(ym_s.sem, 1)
                    dve.wait_ge(mh_s, i * 2 + (j + 1))
                    nc.vector.tensor_tensor(m_lo[:, bass.ds(i * 2 + j, 1), :], ym[:].unsqueeze(1),
                                            m_hi[:, bass.ds(i * 2 + j, 1), :].bitcast(F32), ALU.subtract).then_inc(ml_s.sem, 1)

            tok_banks = [g0, g1, o_bank, misc]

            def out_turn(i, last):
                for j in range(4):
                    if not (last and j == 3):
                        for q in range(4):
                            split_lo(dve, T_OUT, 4, i, j + 1, q)
                for c in range(NCH):
                    dve.wait_ge(tok_p, i * 3 + (c + 1)) if c < NCH - 1 else dense_ready(dve, T_OUT, 4, i, 3)
                    dve.wait_ge(resid_in, 16)
                    cols = y[:, c, bass.ds(i * SEQ, SEQ)]
                    nc.vector.scalar_tensor_tensor(cols, tok_banks[c][:], 0.5, cols, ALU.mult, ALU.add).then_inc(y_add[c].sem, 1)

            with dve.Fori(0, 3) as i:
                out_turn(i, False)
            out_turn(3, True)
            dve.wait_ge(wf_in, 16)
            dve.wait_ge(ysq_s.sem, ysq_s.at(3, 4))
            for c in range(NCH):
                nc.vector.reduce_sum(stot[:, c, 0:1], ssum[:, c, :], AX_X).then_inc(fin_v, 1)
            dve.wait_ge(fin_a, 2)
            for c in range(NCH):
                nc.vector.scalar_tensor_tensor(y[:, c, :], y[:, c, :], stot[:, c, 2:3], wf[:], ALU.mult, ALU.mult)\
                    .then_inc(yn_s, 1)

        @block.tensor
        def _(pe):
            mm = nc.tensor.matmul
            pe.wait_ge(const_in, 48)
            for k in range(KT):
                pe.wait_ge(xsq_done, k + 1)
                mm(misc[:], ones, x_sq[k % 2], start=k == 0, stop=k == KT - 1).then_inc(xsum_done, 1)

            def c_sum(j):
                pe.wait_ge(csq_done, j + 1)
                if j == 0:
                    pe.wait_ge(xrs_done, 1)
                dst = misc if j < CQ else o_bank
                mm(dst[:], ones, c_sq[j % 2], start=j in (0, CQ), stop=j in (CQ - 1, CQ + CK - 1)).then_inc(csum_done, 1)

            for t in range(N_PRE):
                for q in range(4):
                    if t == 0:
                        pe.wait_ge(hl_done, 4 * q + 4)
                    if t >= 2 and q == 0:
                        pe.wait_ge(csq_done, t - 1)
                    dense(pe, 0, 2, 0, t, q)
                    if q == 1 and t >= 1:
                        c_sum(t - 1)

            def qk_sum(i, j):
                pe.wait_ge(cvq_done, i * 2 + (j + 1))
                if not (isinstance(i, int) and i == 0 and j == 0):
                    pe.wait_ge(cvln_done, i * 2 + j)
                mm(misc[:], ones, cv_q[j], start=True, stop=True).then_inc(cvsum_done, 1)

            for q in range(4):
                if q == 0:
                    pe.wait_ge(csq_done, CQ + CK)
                dense(pe, T_QK, 2, 0, 0, q)
            pe.wait_ge(spec_done, 1)
            pe.wait_ge(crs_done, 3)
            mm(misc[:], swap, special, start=True, stop=True).then_inc(swap_done, 1)
            pe.wait_ge(decay_v, 11)
            for c in range(NCH):
                last = nc.tensor.transpose(o_bank[:, c * P:c * P + P], gb[:, c * P:(c + 1) * P], ident)
            last.then_inc(gbt_done, 1)
            pe.wait_ge(kx_done, 1)
            mm(a0[:], fold, k_x, start=True, stop=True).then_inc(fold_done, 1)
            for q in range(4):
                if q == 0:
                    pe.wait_ge(spec_done, 1)
                dense(pe, T_QK, 2, 0, 1, q)
                if q == 2:
                    qk_sum(0, 0)
            with pe.Fori(1, NH) as i:
                for j in range(2):
                    for q in range(4):
                        if q == 0:
                            pe.wait_ge(conv_done, i * 8 + 4 * j - 4)
                        dense(pe, T_QK, 2, i, j, q)
                        if q == 2:
                            qk_sum(i - 1, 1) if j == 0 else qk_sum(i, 0)

            qk_sum(NH - 1, 1)

            with pe.Fori(0, NH) as i:
                def w(s, n):
                    pe.wait_ge(s.sem, s.at(i, n))

                def d(j, *qs):
                    for q in qs:
                        dense(pe, T_HEAD, HEAD_TILES, i, j, q)

                def chunk(ap, c):
                    return ap[:, c * P:(c + 1) * P]

                def level_w(l):
                    w(t_s, l) if l <= 5 else w(ttc_s, 1)
                    if l == 1:
                        w(x_s, 0)
                        w(nat_s, 1)
                    else:
                        w(wc_s, l - 1)
                    for c in range(NCH):
                        ins = mm(chunk(g1, c), chunk(nat, c), chunk(t_mat, c), start=True, stop=True)
                    ins.then_inc(w_s.sem, 1)

                def level_y(l):
                    w(wc_s, l)
                    w(u_s, l + 1)
                    if l == 1:
                        w(attn_s, 1)
                    for c in range(NCH):
                        ins = mm(chunk(g0, c), chunk(w_mat, c), chunk(u_mat, c), start=True, stop=True)
                    ins.then_inc(y_s.sem, 1)

                def scores(b):
                    n = (b + 1) * P
                    dst = a0 if b % 2 == 0 else a1
                    if b >= 2:
                        w(ex_s, b - 1)
                    mm(dst[:, 0:n], chunk(q_n, b), k_n[:, 0:n], start=True, stop=False)
                    mm(dst[:, 0:n], chunk(q_x, b), krope[:, 0:n], start=False, stop=True).then_inc(sc_p.sem, 1)

                def prob_t(b):
                    w(pn_s, b + 1)
                    if b == 0:
                        w(vb_s, 1)
                    else:
                        w(pt_s, b)
                    for n in range(b + 1):
                        ins = nc.tensor.transpose(chunk(misc, n), chunk(prob[b % 2], n), ident)
                    ins.then_inc(pt_p.sem, 1)

                def v_new_product(c):
                    if c == 0:
                        w(u_s, 8)
                        w(vb_s, 1)
                    else:
                        w(x_s, c)
                        w(vn_s, c)
                    rhs = chunk(v_beta, 0) if c == 0 else x_c
                    mm(g0[:, 0:P], chunk(u_mat, c), rhs, start=True, stop=True).then_inc(vn_p.sem, 1)

                def out_and_state(c):
                    w(vn_s, c + 1)
                    if c == 0:
                        w(on_s, 0)
                        w(wc_s, 6)
                    ins = mm(chunk(o_bank, c), v_new, chunk(attn, c), start=c == 0, stop=True)
                    if c == NCH - 1:
                        ins.then_inc(o_p.sem, 1)
                    if c < NCH - 1:
                        mm(g1[:, 0:P], chunk(k_dec, c), v_new, start=True, stop=True).then_inc(up_p.sem, 1)

                def k_state(c):
                    w(st_s, c)
                    mm(g1[:, 0:P], chunk(kbe, c), state, start=True, stop=True).then_inc(ks_p.sem, 1)
                    mm(chunk(o_bank, c), state, chunk(qd, c), start=True, stop=False)

                def up_project(dst, kts, col, c_first, ready, last_inc=None):
                    for n, k in enumerate(range(kts)):
                        sl = slice(col + 256 * k, col + 256 * k + P)
                        ins = three(dst[:], w_hi[ub][:, sl], w_lo[ub][:, sl], c_hi[:, c_first + k, :], c_lo[:, c_first + k, :],
                                    n == 0, n == kts - 1)
                    ins.then_inc(ready.sem, 1)

                ub = (T_HEAD + 1) % 2

                pe.wait_ge(conv_done, 8 * NH - 4)
                w(gate_s, -1)
                d(0, 0)
                w(head_in, 64)
                w(kb_s, 1)
                w(vn_s, 0)
                for c in range(NCH):
                    ins = mm(chunk(g0, c), chunk(kh, c), chunk(kb, c), start=True, stop=True)
                ins.then_inc(kk_s.sem, 1)
                w(oln_s, 0)
                pe.wait_ge(cvln_done, 2 * NH)
                for c in range(NCH):
                    ins = nc.tensor.transpose(chunk(misc, c), chunk(kh, c), ident)
                ins.then_inc(ktr_s.sem, 1)
                d(0, 1)
                w(nat_s, 1)
                for c in range(NCH):
                    ins = mm(chunk(g0, c), chunk(kh, c), chunk(qh, c), start=True, stop=True)
                ins.then_inc(qk_s.sem, 1)
                d(0, 2)
                level_w(1)
                d(0, 3)
                level_y(1)
                split_wait(pe, T_HEAD, HEAD_TILES, i, 1, 3)
                pe.wait_ge(krope_done, 1)
                w(ob_s, 0)
                up_project(a0, CQ, 0, 0, qn_p)
                w(ex_s, 0)
                up_project(a1, CQ, P, 0, qx_p)
                level_w(2)
                w(qn_s, 1)
                up_project(a0, CK, 4 * 256, CQ, kn_p)
                level_y(2)
                w(qx_s, 1)
                for c in range(NCH):
                    for k in range(CK):
                        sl, tok = slice(1024 + 256 * k + P, 1024 + 256 * k + 2 * P), slice(c * P, (c + 1) * P)
                        mm(chunk(a1, c), c_hi[:, CQ + k, tok], w_hi[ub][:, sl], start=k == 0, stop=False)
                        mm(chunk(a1, c), c_lo[:, CQ + k, tok], w_hi[ub][:, sl], start=False, stop=False)
                        ins = mm(chunk(a1, c), c_hi[:, CQ + k, tok], w_lo[ub][:, sl], start=False, stop=k == CK - 1)
                    if c == NCH - 1:
                        ins.then_inc(dense_done, 4)
                w(vconv_s, 4)
                d(2, 0)
                level_w(3)
                d(2, 1)
                level_y(3)
                w(vsil_s, 1)
                w(kdec_s, 1)
                for c in range(NCH):
                    ins = nc.tensor.transpose(chunk(misc, c), chunk(v_sil, c), ident)
                ins.then_inc(vtr_s.sem, 1)
                w(kn_s, 1)
                scores(0)
                d(2, 2)
                level_w(4)
                w(vt_s, 1)
                scores(1)
                d(2, 3)
                level_y(4)
                pe.wait_ge(conv_done, 8 * NH)
                w(gate_s, 0)
                d(3, 0)
                level_w(5)
                prob_t(0)
                scores(2)
                d(3, 1)
                level_y(5)
                prob_t(1)
                scores(3)
                d(3, 2)
                w(u_s, 7)
                w(wc_s, 5)
                for c in range(NCH):
                    ins = nc.tensor.transpose(chunk(g1, c), chunk(u_mat, c), ident)
                ins.then_inc(tt_s.sem, 1)
                d(3, 3)
                level_w(6)
                prob_t(2)
                w(z_s, 1)
                d(4, 0)
                level_y(6)
                prob_t(3)
                d(4, 1)
                v_new_product(0)
                w(pt_s, 4)
                w(ex_s, 3)
                for n in range(NCH):
                    ins = mm(a0[:, n * P:SEQ], chunk(v_tok, n), p_t[:, n, n * P:SEQ], start=n == 0, stop=n == NCH - 1)
                ins.then_inc(pv_p.sem, 1)
                d(4, 2)
                out_and_state(0)
                d(4, 3)
                k_state(1)
                w(z_s, 2)
                d(5, 0)
                v_new_product(1)
                d(5, 1)
                out_and_state(1)
                d(5, 2)
                k_state(2)
                d(5, 3)
                v_new_product(2)
                w(gate_s, 1)
                d(6, 0)
                out_and_state(2)
                d(6, 1)
                k_state(3)
                d(6, 2)
                v_new_product(3)
                d(6, 3)
                out_and_state(3)
                w(gate_s, 2)
                d(7, 0, 1)
                w(osq_s, 1)
                mm(misc[:], ones, o_sq, start=True, stop=True).then_inc(on_p.sem, 1)
                d(7, 2, 3)

            pe.wait_ge(gate_s.sem, gate_s.at(NH - 1, 4))
            with pe.Fori(0, KT // 2) as i:
                for j in range(2):
                    b = (T_MERGE + j) % 2
                    pe.wait_ge(ya_s[j].sem, ya_s[j].at(i, 0))
                    for q in range(4):
                        split_wait(pe, T_MERGE, 2, i, j, q)
                        pe.wait_ge(ol_s, 4 * q + 4)
                        dst = dense_b[b] if q < 2 else (a0, a1)[b]
                        for k in range(4 * q, 4 * q + 4):
                            sl = slice(k * P, (k + 1) * P)
                            ins = three(dst[:], w_hi[b][:, sl], w_lo[b][:, sl], h_hi[:, k, :], h_lo[:, k, :],
                                        k % 8 == 0, k % 8 == 7)
                        ins.then_inc(dense_done, 1)

            tok_banks = [g0, g1, o_bank, misc]
            pe.wait_ge(oln_s.sem, oln_s.at(NH - 1, 1))
            pe.wait_ge(on_s.sem, on_s.at(NH - 1, 1))
            pe.wait_ge(x_s.sem, x_s.at(NH - 1, 3))
            pe.wait_ge(vn_s.sem, vn_s.at(NH - 1, 4))
            with pe.Fori(0, 4) as i:
                for j in range(4):
                    b = (T_OUT + j) % 2
                    split_wait(pe, T_OUT, 4, i, j, 3)
                    pe.wait_ge(ml_s.sem, ml_s.base + 4 * j + 4)
                    for c in range(NCH):
                        if j == 0:
                            pe.wait_ge(y_add[c].sem, y_add[c].at(i, 0))
                        for k in range(4):
                            r, tok, sl = 4 * j + k, slice(c * P, (c + 1) * P), slice(k * SEQ, (k + 1) * SEQ)
                            last = c == NCH - 1
                            ins = [mm(tok_banks[c][:], m_hi[:, r, tok], w_hi[b][:, sl], start=r == 0, stop=False),
                                   mm(tok_banks[c][:], m_hi[:, r, tok], w_lo[b][:, sl], start=False, stop=False),
                                   mm(tok_banks[c][:], m_lo[:, r, tok], w_hi[b][:, sl], start=False, stop=r == KT - 1)]
                            if j == 3 and k == 3 and not last:
                                ins[2].then_inc(tok_p, 1)
                    ins[2].then_inc(dense_done, 4)


def weight_tiles(w_in, w_uq, w_ukv, proj_a, proj_b, w_out):
    def rows(w):
        return w.reshape(-1, P, w.shape[1]).transpose(1, 0, 2)

    at = np.cumsum([0, 3 * NH * P, NH * P, NH, NH, Q_RANK, KV_RANK, ROPE, NH * P, D_MODEL])
    qkv, z_a, alpha, beta, c_q, c_kv, k_rope, z_b, gates = (int(n) for n in at[:9])

    def columns(c0):
        return w_in[:, c0:c0 + P]

    special = np.zeros((D_MODEL, P), w_in.dtype)
    special[:, 0:NH] = w_in[:, alpha:alpha + NH]
    special[:, 32:32 + NH] = w_in[:, beta:beta + NH]
    special[:, 64:64 + ROPE] = w_in[:, k_rope:k_rope + ROPE]
    tiles = [rows(columns(c_q + n * P)) for n in range(CQ)] + [rows(columns(c_kv + n * P)) for n in range(CK)]
    tiles.append(rows(special))
    for h in range(NH):
        tiles += [rows(columns(qkv + h * P)), rows(columns(qkv + (NH + h) * P))]
    for h in range(NH):
        u = w_uq[:, h * 192:(h + 1) * 192]
        x1, x2 = u[:, P:P + 32], u[:, P + 32:P + 64]
        uq = rows(np.concatenate([u[:, 0:P], x1, x2, x2, x1], axis=1)).reshape(P, -1)
        ukv = rows(w_ukv[:, h * 256:(h + 1) * 256]).reshape(P, -1)
        pad = np.zeros((P, TILE - uq.shape[1] - ukv.shape[1]), w_in.dtype)
        tiles.append(rows(columns(qkv + (2 * NH + h) * P)))
        tiles.append(np.concatenate([uq, ukv, pad], axis=1))
        tiles += [rows(columns(z_b + h * P)), rows(columns(z_a + h * P))]
        tiles += [rows(columns(gates + (4 * h + n) * P)) for n in range(4)]
    for f in range(KT):
        sl = slice(f * P, (f + 1) * P)
        tiles.append(np.concatenate([rows(proj_a[:, sl]), rows(proj_b[:, sl])], axis=1))
    for n in range(4):
        for g in range(4):
            tiles.append(rows(w_out[g * SEQ:(g + 1) * SEQ, n * SEQ:(n + 1) * SEQ]))
    return np.ascontiguousarray(np.stack([t.reshape(P, TILE) for t in tiles]))


def constants():
    p = np.arange(P)
    c = np.zeros((P, N_CONST), np.float32)
    c[:, C_IDENT:C_IDENT + P] = np.eye(P)
    for n in range(ROPE):
        c[64 + n, C_SWAP + n] = 1
        c[64 + n, C_SWAP + 64 + (n + 32) % 64] = 1
    c[:, C_FOLD:C_FOLD + P] = p[:, None] % 64 == p[None, :] % 64
    c[:, C_ONES:C_ONES + P] = 1
    c[:, C_MASKQ:C_MASKQ + P] = np.where(p[None, :] <= p[:, None], 0, NEG)
    c[:, C_MASKG:C_MASKG + P] = np.where(p[None, :] >= p[:, None], 0, NEG)
    c[:, C_FREQ] = (10000.0 ** (-np.arange(0, ROPE, 2) / ROPE))[p % 32]
    turn = np.array([0.25, 0.25, 0.5, 0.0])[p // 32]
    c[:, C_TURN], c[:, C_TURN2PI], c[:, C_EPS] = turn, turn * 2 * math.pi, EPS
    m = np.zeros((P, 7, P), np.int32)
    j, i = p[:, None], p[None, :]
    for n in range(7):
        b = 1 << n
        m[:, n, :] = (i // (2 * b) == j // (2 * b)) & (i // b == j // b + 1)
    return c, m.reshape(P, 7 * P)


def kernel(x, positions, norm_w, w_in, conv_w, a_log, dt_bias, gdn_norm_w, q_norm_w, w_uq, kv_norm_w,
           w_ukv, proj_a, proj_b, w_out, final_norm_w):
    import concourse.bacc as bacc
    from concourse.bass_utils import run_bass_kernel_spmd

    (x, positions, norm_w, w_in, conv_w, a_log, dt_bias, gdn_norm_w, q_norm_w, w_uq, kv_norm_w, w_ukv, proj_a,
     proj_b, w_out, final_norm_w) = (np.asarray(a) for a in (
         x, positions, norm_w, w_in, conv_w, a_log, dt_bias, gdn_norm_w, q_norm_w, w_uq, kv_norm_w, w_ukv, proj_a,
         proj_b, w_out, final_norm_w))
    xs = np.ascontiguousarray(x[0])
    params = np.zeros((P, N_PARAM), np.float32)
    params[:, P_NORM:P_NORM + KT] = norm_w[0].reshape(KT, P).T
    params[:, P_QN:P_QN + CQ] = q_norm_w[0].reshape(CQ, P).T
    params[:, P_KVN:P_KVN + CK] = kv_norm_w[0].reshape(CK, P).T
    params[:, P_GN] = gdn_norm_w[0]
    params[:, P_CONV:P_CONV + 96] = conv_w[0].reshape(4, 24, P).transpose(2, 1, 0).reshape(P, 96)
    params[0:NH, P_DT], params[0:NH, P_ALOG] = dt_bias[0], a_log[0]
    consts, masks = constants()
    arrays = {
        "xt": np.ascontiguousarray(xs.T.reshape(KT, P, SEQ).transpose(1, 0, 2)),
        "x": xs, "positions": np.ascontiguousarray(positions), "params": params,
        "wfinal": final_norm_w.reshape(1, D_MODEL),
        "stream": weight_tiles(w_in[0], w_uq[0], w_ukv[0], proj_a[0], proj_b[0], w_out[0]),
        "consts": consts, "masks": masks,
    }
    nc = bacc.Bacc("TRN2", target_bir_lowering=False, num_devices=1)
    aps = {n: nc.dram_tensor(f"in_{n}", a.shape, mybir.dt.from_np(a.dtype), kind="ExternalInput").ap()
           for n, a in arrays.items()}
    out = nc.dram_tensor("out", (SEQ, D_MODEL), F32, kind="ExternalOutput").ap()
    program(nc, **aps, out=out)
    r = run_bass_kernel_spmd(nc, [{f"in_{n}": a for n, a in arrays.items()}], core_ids=[0])
    return r.results[0]["out"].reshape(1, SEQ, D_MODEL)
```

```python
import math
from contextlib import ExitStack

import numpy as np

import concourse.bass as bass
from concourse import mybir

P = 128
D_MODEL, SEQ = 2048, 512
KT = D_MODEL // P
NH = 8
Q_RANK, KV_RANK, ROPE = 512, 256, 64
CQ, CK = Q_RANK // P, KV_RANK // P
NCH = SEQ // P
EPS = 1e-6
SCALE = 1.0 / math.sqrt(128 + ROPE)
TILE = 2048
QT = TILE // 4

T_PRE = 0
N_PRE = CQ + CK + 1
T_QK = T_PRE + N_PRE
T_HEAD = T_QK + 2 * NH
HEAD_TILES = 8
T_MERGE = T_HEAD + HEAD_TILES * NH
T_OUT = T_MERGE + KT
N_TILES = T_OUT + 16

F32, F32R = mybir.dt.float32, mybir.dt.float32r
I32, U8 = mybir.dt.int32, mybir.dt.uint8
ALU, ACT = mybir.AluOpType, mybir.ActivationFunctionType
AX_X = mybir.AxisListType.X

C_IDENT, C_SWAP, C_FOLD, C_ONES, C_MASKQ, C_MASKG = (n * P for n in range(6))
C_FREQ, C_TURN, C_TURN2PI, C_EPS = (6 * P + n for n in range(4))
N_CONST = 6 * P + 4
P_NORM, P_QN, P_KVN, P_GN = 0, KT, KT + CQ, KT + CQ + CK
P_CONV = P_GN + 1
P_DT = P_CONV + 24 * 4
P_ALOG = P_DT + 1
N_PARAM = P_ALOG + 1
NEG = -1e30
HALF = D_MODEL // 2
N_O = 6


class Signal:

    def __init__(self, sem, per_turn, base=0):
        self.sem, self.per_turn, self.base = sem, per_turn, base

    def at(self, i, n):
        return i * self.per_turn + (self.base + n)


def program(nc, xt, x, positions, params, wfinal, stream, consts, masks, out):
    qk_dram = nc.dram_tensor("qk_scratch", [2 * NH, P, SEQ], F32, kind="Internal").ap()
    gb_dram = nc.dram_tensor("gb_scratch", [2 * NH, SEQ], F32, kind="Internal").ap()
    gate_dram = nc.dram_tensor("gate_scratch", [2 * KT, P, SEQ], F32, kind="Internal").ap()
    base_dram = nc.dram_tensor("base_scratch", [64, 16], F32, kind="Internal").ap()
    o_dram = nc.dram_tensor("o_scratch", [2 * NH, P, SEQ], F32, kind="Internal").ap()

    ctx = ExitStack()
    with ctx:
        base = (nc.sbuf_base + 63) // 64 * 64
        at = [base]

        def place(name, shape, dt, size=4, offset=None):
            n = int(np.prod(shape[1:])) * size
            if offset is None:
                offset = at[0]
                at[0] += (n + 63) // 64 * 64
            return nc.alloc_sbuf_tensor_at(name, shape, dt, offset=offset)

        w_raw = [place(f"w_raw{b}", [P, TILE], F32) for b in range(2)]
        w_hi = [place(f"w_hi{b}", [P, TILE], F32R) for b in range(2)]
        w_lo = [place(f"w_lo{b}", [P, TILE], F32R) for b in range(2)]
        const = place("const", [P, N_CONST], F32)
        param = place("param", [P, N_PARAM], F32)
        lmask = place("lmask", [P, 7, P], U8, 1)
        krope = place("krope", [P, SEQ], F32)
        cs = place("cs", [P, SEQ], F32)
        gball = place("gball", [P, NH, 8], F32)
        h_off = at[0]
        h_hi = place("h_hi", [P, KT, SEQ], F32R)
        h_lo = place("h_lo", [P, KT, SEQ], F32R)
        c_off = at[0]
        c_hi = place("c_hi", [P, CQ + CK, SEQ], F32R)
        c_lo = place("c_lo", [P, CQ + CK, SEQ], F32R)
        n_slots = (nc.sbuf_top - at[0] - 64) // (SEQ * 4)
        slots = place("slots", [P, n_slots, SEQ], F32)
        assert n_slots >= 31, n_slots
        m_hi = place("m_hi", [P, KT, SEQ], F32R, offset=c_off)
        m_lo = place("m_lo", [P, KT, SEQ], F32R, offset=c_off + KT * SEQ * 4)
        t_off = c_off + 2 * KT * SEQ * 4
        gate_in = place("gate_in", [P, 2, 2, SEQ], F32, offset=t_off)
        ya = place("ya", [P, SEQ], F32, offset=t_off + 8192)
        yb = place("yb", [P, SEQ], F32, offset=t_off + 10240)
        ym = place("ym", [P, SEQ], F32, offset=t_off + 12288)
        o_in = place("o_in", [P, N_O, SEQ], F32, offset=t_off + 8192)
        assert t_off + 8192 + N_O * 2048 <= nc.sbuf_top
        y = place("y", [P, NCH, D_MODEL], F32, offset=h_off)
        wf = place("wf", [P, D_MODEL], F32, offset=h_off + NCH * D_MODEL * 4)
        ysq = place("ysq", [P, SEQ], F32, offset=h_off + NCH * D_MODEL * 4 + 8192)
        ssum = place("ssum", [P, NCH, 4], F32, offset=h_off + NCH * D_MODEL * 4 + 8192 + 2048)
        stot = place("stot", [P, NCH, 4], F32, offset=h_off + NCH * D_MODEL * 4 + 8192 + 2112)

        def slot(n):
            return slots[:, n, :]

        def blocks(ap):
            return ap.rearrange("p (c n) -> p c n", c=NCH)

        ident, swap = const[:, C_IDENT:C_IDENT + P], const[:, C_SWAP:C_SWAP + P]
        fold, ones = const[:, C_FOLD:C_FOLD + P], const[:, C_ONES:C_ONES + P]
        mask_q, mask_g = const[:, C_MASKQ:C_MASKQ + P], const[:, C_MASKG:C_MASKG + P]
        eps = const[:, C_EPS:C_EPS + 1]

        xs = [slot(k) for k in range(KT)]
        x_sq, x_ln, x_rs, h_tmp = [slot(16), slot(17)], slot(18), slot(19), [slot(20), slot(21)]
        x_sq2 = h_tmp
        c_raw = [slot(22 + j) for j in range(6)]
        c_sq = [slot(28), slot(29)]
        mask_i = slots[:, 28:30, :].rearrange("p a n -> p (a n)")[:, 0:7 * P].bitcast(I32)
        special, pos_f, ang, turns = slot(18), slot(0), slot(1), slot(2)
        pos_i = slot(4).bitcast(I32)
        gb = slot(5)
        g_abs, g_sp, g_ex, g_ln = slot(6), slot(7), slot(8), slot(3)
        k_x = slot(9)
        c_ln, c_rs, c_tmp = slot(10), [slot(11), slot(12)], [slot(13), slot(14)]
        cv, cv_e, cv_s, cv_q = ([slot(n), slot(n + 1)] for n in (15, 17, 19, 21))
        cv_ln, cv_rs, cv_o = slot(23), slot(24), [slot(25), slot(29)]
        (qh, kh, g_bc, b_bc, kb, e_mat, e_g, kbe, qd, nat, u_mat, t_mat, w_mat, attn, k_dec,
         v_conv, z_a, z_b, z_e, gate_o0, q_n, q_x, k_n, v_tok, prob0, prob1) = (slot(n) for n in range(26))
        prob, gate_o = [prob0, prob1], [gate_o0, z_e]
        p_t = slots[:, 26:30, :]
        rec = slot(30)
        x_c, v_new, state = rec[:, 0:P], rec[:, P:2 * P], rec[:, 2 * P:3 * P]
        small = rec[:, 3 * P:4 * P]
        hs = small[:, 0:8]
        sc_max, sc_nb, sc_sum, sc_r = (small[:, 8 + 4 * n:12 + 4 * n] for n in range(4))
        a_neg = small[0:NH, 32:33]
        dg, v_e, v_sil, v_beta = e_mat, e_mat, v_conv, v_conv
        o_sq, o_ln, o_rs, o_n, o_a, o_b = w_mat, nat, t_mat, kb, q_n, q_x

        bank = [ctx.enter_context(nc.psum_tensor(f"bank{n}", [P, SEQ], F32)) for n in range(8)]
        dense_b = bank[0:2]
        g0, g1, o_bank, misc, a0, a1 = bank[2:8]

        def sem(name):
            return ctx.enter_context(nc.semaphore(name))

        based = []

        def sig(name, per_turn, base=0):
            s = Signal(sem(name), per_turn, base)
            if base:
                based.append(s)
            return s

        raw_in = [sem(f"raw_in{b}") for b in range(2)]
        hi_done, lo_done = sem("hi_done"), sem("lo_done")
        dense_done = sem("dense_done")

        def tile_of(base_t, per, i, j):
            assert per % 2 == 0
            return (base_t + j) % 2, i * per + (base_t + j)

        def load_tile(sp, base_t, per, i, j):
            b, t = tile_of(base_t, per, i, j)
            sp.wait_ge(lo_done, i * 4 * per + 4 * (base_t + j - 1)) if base_t + j >= 2 else None
            sp.dma_start(w_raw[b][:], stream[t]).then_inc(raw_in[b], 16)

        def split_hi(act, base_t, per, i, j, q):
            b = (base_t + j) % 2
            if q == 0:
                act.wait_ge(raw_in[b], i * 8 * per + 16 * ((base_t + j) // 2 + 1))
            if base_t + j >= 2:
                act.wait_ge(dense_done, i * 4 * per + 4 * (base_t + j - 2) + q + 1)
            sl = slice(q * QT, (q + 1) * QT)
            nc.scalar.copy(w_hi[b][:, sl], w_raw[b][:, sl]).then_inc(hi_done, 1)

        def split_lo(dve, base_t, per, i, j, q, on=nc.vector):
            b = (base_t + j) % 2
            dve.wait_ge(hi_done, i * 4 * per + 4 * (base_t + j) + q + 1)
            sl = slice(q * QT, (q + 1) * QT)
            on.tensor_tensor(w_lo[b][:, sl], w_raw[b][:, sl], w_hi[b][:, sl].bitcast(F32),
                             ALU.subtract).then_inc(lo_done, 1)

        def split_wait(pe, base_t, per, i, j, q):
            pe.wait_ge(lo_done, i * 4 * per + 4 * (base_t + j) + q + 1)

        def three(dst, a_hi, a_lo, b_hi, b_lo, start, stop):
            nc.tensor.matmul(dst, a_hi, b_hi, start=start, stop=False)
            nc.tensor.matmul(dst, a_hi, b_lo, start=False, stop=False)
            return nc.tensor.matmul(dst, a_lo, b_hi, start=False, stop=stop)

        def dense(pe, base_t, per, i, j, q):
            b = (base_t + j) % 2
            split_wait(pe, base_t, per, i, j, q)
            for k in range(4 * q, 4 * q + 4):
                sl = slice(k * P, (k + 1) * P)
                mm = three(dense_b[b][:], w_hi[b][:, sl], w_lo[b][:, sl], h_hi[:, k, :], h_lo[:, k, :],
                           k == 0, k == KT - 1)
            mm.then_inc(dense_done, 1)

        def dense_ready(eng, base_t, per, i, j):
            eng.wait_ge(dense_done, i * 4 * per + 4 * (base_t + j) + 4)

        mask_done = sem("mask_done")
        const_in, param_in, mask_in, pos_in = sem("const_in"), sem("param_in"), sem("mask_in"), sem("pos_in")
        x_in = [sem(f"x_in{n}") for n in range(KT // 2)]
        xsq_v, xpair_done = sem("xsq_v"), sem("xpair_done")
        xsq_done, xsum_done, xrs_done = sem("xsq_done"), sem("xsum_done"), sem("xrs_done")
        hm_done, hh_done, hl_done = sem("hm_done"), sem("hh_done"), sem("hl_done")
        craw_done, csq_done, csum_done, crs_done = sem("craw_done"), sem("csq_done"), sem("csum_done"), sem("crs_done")
        cm_done, ch_done, cl_done = sem("cm_done"), sem("ch_done"), sem("cl_done")
        spec_done, rope_v, cs_done, decay_v, decay_a = (sem(n) for n in ("spec_done", "rope_v", "cs_done", "decay_v", "decay_a"))
        gbt_done, gball_done, gb_stored = sem("gbt_done"), sem("gball_done"), sem("gb_stored")
        swap_done, kx_done, fold_done, krope_done = sem("swap_done"), sem("kx_done"), sem("fold_done"), sem("krope_done")
        conv_done, cve_done, cvs_done, cvq_done = sem("conv_done"), sem("cve_done"), sem("cvs_done"), sem("cvq_done")
        cvsum_done, cvln_done, cvrs_done, cvo_done = sem("cvsum_done"), sem("cvln_done"), sem("cvrs_done"), sem("cvo_done")
        qk_stored = [sig("q_stored", 16, 16), sig("k_stored", 16, 16)]
        head_in = sig("head_in", 64)
        kb_s, hs_s, dg_s, e_s, eg_s, dec_s = sig("kb_s", 1), sig("hs_s", 1), sig("dg_s", 4), sig("e_s", 1), sig("eg_s", 1), sig("dec_s", 2)
        kk_s, ktr_s, qk_s, nat_s, kdec_s, attn_s = (sig(n, 1) for n in ("kk_s", "ktr_s", "qk_s", "nat_s", "kdec_s", "attn_s"))
        u_s, t_s, w_s, wc_s, y_s, tt_s, ttc_s = sig("u_s", 8), sig("t_s", 5), sig("w_s", 6), sig("wc_s", 6), sig("y_s", 6, 1), sig("tt_s", 1), sig("ttc_s", 1)
        vconv_s, vtanh_s, vsil_s, vtr_s, vb_s = sig("vconv_s", 4), sig("vtanh_s", 1), sig("vsil_s", 1), sig("vtr_s", 1), sig("vb_s", 1)
        ze_s, z_s, gate_s = sig("ze_s", 2), sig("z_s", 2), sig("gate_s", 4, 2)
        gate_st = [sig("gate_st_even", 32, 16), sig("gate_st_odd", 32, 16)]
        qn_p, qx_p, kn_p = (sig(n, 1) for n in ("qn_p", "qx_p", "kn_p"))
        qn_s, qx_s, kn_s, vt_s = (sig(n, 1) for n in ("qn_s", "qx_s", "kn_s", "vt_s"))
        sc_p, msk_s, max_s, nb_s, rc_s, pn_s = (sig(n, 4) for n in ("sc_p", "msk_s", "max_s", "nb_s", "rc_s", "pn_s"))
        ex_s = sig("ex_s", 4, 1)
        pt_p, pt_s = sig("pt_p", 4), sig("pt_s", 4)
        pv_p, ob_s = sig("pv_p", 1, 1), sig("ob_s", 1, 1)
        ks_p, x_s, vn_p, vn_s, up_p, st_s = sig("ks_p", 3), sig("x_s", 3, 1), sig("vn_p", 4), sig("vn_s", 4, 1), sig("up_p", 3), sig("st_s", 3)
        o_p, on_p, oln_s, on_s, oa_s = (sig(n, 1, 1) for n in ("o_p", "on_p", "oln_s", "on_s", "oa_s"))
        osq_s, ors_s = sig("osq_s", 1), sig("ors_s", 1)
        o_st = sig("o_st", 32, 16)
        o_in_s, oh_s, ol_s = [sem(f"o_in_s{n}") for n in range(N_O)], sem("oh_s"), sem("ol_s")
        gate_ld = [sem("gate_ld0"), sem("gate_ld1")]
        ya_s, ym_s, mh_s, ml_s = [sig("ya_s0", 2, 1), sig("ya_s1", 2, 1)], sig("ym_s", 2, 1), sem("mh_s"), sig("ml_s", 2, 1)
        resid_in, wf_in = sem("resid_in"), sem("wf_in")
        tok_p, y_add, ysq_s = sem("tok_p"), [sig(f"y_add{c}", 1, 1) for c in range(NCH)], sig("ysq_s", 4, 1)
        fin_v, fin_a, yw_s, yn_s, yn_a, out_st = (sem(n) for n in ("fin_v", "fin_a", "yw_s", "yn_s", "yn_a", "out_st"))

        block = ctx.enter_context(nc.Block())

        @block.sync
        def _(sp):
            sp.dma_start(const[:], consts).then_inc(const_in, 16)
            for n in range(KT // 2):
                sp.dma_start(slots[:, 2 * n:2 * n + 2, :], xt[:, 2 * n:2 * n + 2, :]).then_inc(x_in[n], 16)
            sp.dma_start(param[:], params).then_inc(param_in, 16)
            load_tile(sp, T_PRE, 2, 0, 0)
            load_tile(sp, T_PRE, 2, 0, 1)
            sp.dma_start(mask_i, masks).then_inc(mask_in, 16)
            for t in range(2, T_QK + 2):
                load_tile(sp, T_PRE, 2, 0, t)
            with sp.Fori(1, NH) as i:
                for j in range(2):
                    load_tile(sp, T_QK, 2, i, j)
            with sp.Fori(0, NH) as i:
                for j in range(HEAD_TILES):
                    load_tile(sp, T_HEAD, HEAD_TILES, i, j)
            with sp.Fori(0, KT // 2) as i:
                for j in range(2):
                    load_tile(sp, T_MERGE, 2, i, j)
            with sp.Fori(0, 4) as i:
                for j in range(4):
                    load_tile(sp, T_OUT, 4, i, j)
            for c in range(NCH):
                sp.wait_ge(yn_a, c + 1)
                sp.dma_start(out[c * P:(c + 1) * P, 0:HALF], y[:, c, 0:HALF]).then_inc(out_st, 16)
                sp.wait_ge(yn_s, 2 * c + 2)
                sp.dma_start(out[c * P:(c + 1) * P, HALF:D_MODEL], y[:, c, HALF:D_MODEL]).then_inc(out_st, 16)
            sp.wait_ge(out_st, 32 * NCH)

        @block.gpsimd
        def _(pool):
            for n, s in enumerate(based):
                if s.base % 16 == 0:
                    pool.dma_start(base_dram[n:n + 1, :], consts[n:n + 1, 0:16]).then_inc(s.sem, 16)
                else:
                    pool.sem_inc(s.sem, s.base)
            for t in range(2):
                for q in range(4):
                    split_lo(pool, 0, 2, 0, t, q, on=nc.gpsimd)
            pool.wait_ge(hm_done, KT)
            pool.dma_start(pos_i, positions.to_broadcast([P, SEQ])).then_inc(pos_in, 16)
            pool.wait_ge(decay_v, 11)
            pool.dma_start(gb_dram[0:NH, :], gb[0:NH, :]).then_inc(gb_stored, 16)
            pool.dma_start(gb_dram[NH:2 * NH, :], gb[32:32 + NH, :]).then_inc(gb_stored, 16)
            def store_qk(i):
                for j in range(2):
                    pool.wait_ge(cvo_done, i * 2 + (j + 1))
                    pool.dma_start(qk_dram[i * 2 + j], cv_o[j]).then_inc(qk_stored[j].sem, 16)

            def load_head(i):
                pool.dma_start(qh, qk_dram[i * 2]).then_inc(head_in.sem, 16)
                pool.dma_start(kh, qk_dram[i * 2 + 1]).then_inc(head_in.sem, 16)
                pool.dma_start(g_bc, gb_dram[bass.ds(i, 1), :].to_broadcast([P, SEQ])).then_inc(head_in.sem, 16)
                pool.dma_start(b_bc, gb_dram[bass.ds(i + NH, 1), :].to_broadcast([P, SEQ])).then_inc(head_in.sem, 16)

            pool.wait_ge(cl_done, CQ + CK)
            pool.wait_ge(krope_done, 1)
            pool.wait_ge(gball_done, 2)
            pool.wait_ge(cs_done, 1)
            pool.wait_ge(gb_stored, 32)
            store_qk(0)
            for j in range(2):
                pool.wait_ge(qk_stored[j].sem, qk_stored[j].at(0, 16))
            load_head(0)
            with pool.Fori(1, NH) as i:
                store_qk(i)
            for j in range(2):
                pool.wait_ge(qk_stored[j].sem, qk_stored[j].at(NH - 1, 16))

            def head_stores(i):
                pool.wait_ge(ob_s.sem, ob_s.at(i, 1))
                pool.dma_start(o_dram[i], o_b).then_inc(o_st.sem, 16)
                for n in range(4):
                    if n == 3:
                        pool.wait_ge(oa_s.sem, oa_s.at(i, 1))
                        pool.dma_start(o_dram[i + NH], o_a).then_inc(o_st.sem, 16)
                    pool.wait_ge(gate_s.sem, gate_s.at(i, n + 1))
                    pool.dma_start(gate_dram[i * 4 + n], gate_o[n % 2]).then_inc(gate_st[n % 2].sem, 16)

            with pool.Fori(0, NH - 1) as i:
                pool.wait_ge(qk_s.sem, qk_s.at(i, 1))
                pool.wait_ge(ktr_s.sem, ktr_s.at(i, 1))
                pool.wait_ge(dec_s.sem, dec_s.at(i, 2))
                load_head(i + 1)
                head_stores(i)

            def load_o(n):
                pool.dma_start(o_in[:, n % N_O, :], o_dram[n]).then_inc(o_in_s[n % N_O], 16)

            pool.wait_ge(pv_p.sem, pv_p.at(NH - 1, 1))
            pool.wait_ge(o_st.sem, o_st.at(NH - 1, 0))
            for n in range(N_O):
                load_o(n)
            head_stores(NH - 1)

            pool.wait_ge(o_st.sem, o_st.at(NH - 1, 32))
            for n in range(N_O, 2 * NH):
                pool.wait_ge(ol_s, n - N_O + 1)
                load_o(n)
            for p in range(2):
                pool.wait_ge(gate_st[p].sem, gate_st[p].at(NH - 1, 32))

            def load_gates(f, p):
                pool.dma_start(gate_in[:, p, 0, :], gate_dram[f + KT]).then_inc(gate_ld[p], 16)
                pool.dma_start(gate_in[:, p, 1, :], gate_dram[f]).then_inc(gate_ld[p], 16)

            load_gates(0, 0)
            load_gates(1, 1)
            with pool.Fori(0, KT // 2 - 1) as i:
                for p in range(2):
                    pool.wait_ge(ya_s[p].sem, ya_s[p].at(i, 2))
                    load_gates(i * 2 + (2 + p), p)
            pool.wait_ge(dense_done, 4 * T_OUT)
            pool.dma_start(y[:], x.rearrange("(c p) d -> p c d", p=P)).then_inc(resid_in, 16)
            pool.dma_start(wf[:], wfinal.to_broadcast([P, D_MODEL])).then_inc(wf_in, 16)

        @block.scalar
        def _(act):
            nc.scalar.preload_act_table_set("natural_log_exp_and_others")
            for n in range(KT // 2):
                act.wait_ge(x_in[n], 16)
                if n >= 2:
                    act.wait_ge(xpair_done, n - 1)
                nc.scalar.activation(x_sq[n % 2], xs[2 * n], ACT.Square).then_inc(xsq_done, 1)
            act.wait_ge(const_in, 16)
            act.wait_ge(param_in, 16)
            act.wait_ge(xsum_done, KT // 2)
            nc.scalar.activation(x_ln, misc[:], ACT.Ln, bias=eps, scale=1.0 / D_MODEL).then_inc(xrs_done, 1)
            act.wait_ge(xrs_done, 1)
            nc.scalar.activation(x_rs, x_ln, ACT.Exp, scale=-0.5).then_inc(xrs_done, 1)
            pending = [(t, q) for t in range(2) for q in range(4)]
            for k in range(KT):
                for t, q in [pending.pop(0)] if pending else []:
                    split_hi(act, 0, 2, 0, t, q)
                act.wait_ge(hm_done, k + 1)
                nc.scalar.copy(h_hi[:, k, :], h_tmp[k % 2]).then_inc(hh_done, 1)

            for t in range(CQ + CK):
                for q in range(4):
                    if t != 1:
                        split_hi(act, 0, 2, 0, max(t + 1, 2), q)
                dense_ready(act, 0, 2, 0, t)
                nc.scalar.copy(c_raw[t], dense_b[t % 2][:]).then_inc(craw_done, 1)
                act.wait_ge(mask_done, 1)
                if t >= 2:
                    act.wait_ge(csum_done, t - 1)
                nc.scalar.activation(c_sq[t % 2], dense_b[t % 2][:], ACT.Square).then_inc(csq_done, 1)
            for q in range(4):
                split_hi(act, 0, 2, 0, N_PRE, q)
            for n, (bank_c, width, count) in enumerate(((misc, Q_RANK, CQ), (o_bank, KV_RANK, CQ + CK))):
                act.wait_ge(csum_done, count)
                if n:
                    act.wait_ge(crs_done, 2)
                nc.scalar.activation(c_ln, bank_c[:], ACT.Ln, bias=eps, scale=1.0 / width).then_inc(crs_done, 1)
                act.wait_ge(crs_done, 2 * n + 1)
                nc.scalar.activation(c_rs[n], c_ln, ACT.Exp, scale=-0.5).then_inc(crs_done, 1)
            for j in range(CQ + CK):
                act.wait_ge(cm_done, j + 1)
                nc.scalar.copy(c_hi[:, j, :], c_tmp[j % 2]).then_inc(ch_done, 1)
            dense_ready(act, 0, 2, 0, N_PRE - 1)
            nc.scalar.copy(special, dense_b[(N_PRE - 1) % 2][:]).then_inc(spec_done, 1)
            act.wait_ge(decay_v, 2)
            nc.scalar.activation(g_ex[0:NH, :], g_abs[0:NH, :], ACT.Exp, scale=-1.0).then_inc(decay_a, 1)
            act.wait_ge(decay_a, 1)
            nc.scalar.activation(g_ln[0:NH, :], g_ex[0:NH, :], ACT.Ln, bias=ones[0:NH, 0:1]).then_inc(decay_a, 1)
            nc.scalar.activation(g_ex[32:32 + NH, :], special[32:32 + NH, :], ACT.Tanh, scale=0.5).then_inc(decay_a, 1)
            nc.scalar.activation(a_neg, param[0:NH, P_ALOG:P_ALOG + 1], ACT.Exp).then_inc(decay_a, 1)
            act.wait_ge(rope_v, 8)
            nc.scalar.activation(cs[:], ang, ACT.Sin).then_inc(cs_done, 1)

            def silu_tanh(i, j):
                act.wait_ge(conv_done, i * 8 + 4 * j + 4)
                nc.scalar.activation(cv_e[j], cv[j], ACT.Tanh, scale=0.5).then_inc(cve_done, 1)

            def square(i, j):
                act.wait_ge(cvs_done, i * 2 + (j + 1))
                nc.scalar.activation(cv_q[j], cv_s[j], ACT.Square).then_inc(cvq_done, 1)

            def norm_factor(n, j):
                act.wait_ge(cvsum_done, n + 1)
                if not (isinstance(n, int) and n == 0):
                    act.wait_ge(cvo_done, n)
                nc.scalar.activation(cv_ln, misc[:], ACT.Ln, bias=eps, scale=0.25).then_inc(cvln_done, 1)
                act.wait_ge(cvln_done, n + 1)
                nc.scalar.activation(cv_rs, cv_ln, ACT.Exp, scale=-0.5).then_inc(cvrs_done, 1)

            for q in range(4):
                split_hi(act, T_QK, 2, 0, 1, q)

            def qk_turn(i, last=False):
                for j in range(2):
                    def hi(*qs):
                        if not (last and j == 1):
                            for q in qs:
                                split_hi(act, T_QK, 2, i, j + 2, q)
                    hi(0, 1)
                    silu_tanh(i, j)
                    hi(2)
                    square(i, j)
                    hi(3)
                    norm_factor(i * 2 + j, j)

            qk_turn(0)
            with act.Fori(1, NH - 1) as i:
                qk_turn(i)
            qk_turn(NH - 1, True)

            with act.Fori(0, NH) as i:
                def hi(j, *qs):
                    for q in qs:
                        split_hi(act, T_HEAD, HEAD_TILES, i, j, q)

                def w_copy(l):
                    act.wait_ge(w_s.sem, w_s.at(i, l))
                    act.wait_ge(y_s.sem, y_s.at(i, l - 1))
                    nc.scalar.copy(w_mat, g1[:]).then_inc(wc_s.sem, 1)

                def exp_scores(b):
                    n = (b + 1) * P
                    src = a0 if b % 2 == 0 else a1
                    act.wait_ge(nb_s.sem, nb_s.at(i, b + 1))
                    if b >= 2:
                        act.wait_ge(pt_p.sem, pt_p.at(i, b - 1))
                    nc.scalar.activation(prob[b % 2][:, 0:n], src[:, 0:n], ACT.Exp, bias=sc_nb[:, b:b + 1],
                                         scale=SCALE, accum_out=sc_sum[:, b:b + 1]).then_inc(ex_s.sem, 1)

                def pt_copy(b):
                    act.wait_ge(pt_p.sem, pt_p.at(i, b + 1))
                    if b == 0:
                        act.wait_ge(pv_p.sem, pv_p.at(i, 0))
                    nc.scalar.copy(p_t[:, 0:b + 1, b * P:(b + 1) * P], blocks(misc[:])[:, 0:b + 1, :])\
                        .then_inc(pt_s.sem, 1)

                def z_tanh(n, j):
                    dense_ready(act, T_HEAD, HEAD_TILES, i, j)
                    if n == 0:
                        act.wait_ge(gate_st[1].sem, gate_st[1].at(i, 0))
                    else:
                        act.wait_ge(z_s.sem, z_s.at(i, 1))
                    nc.scalar.activation(z_e, dense_b[(T_HEAD + j) % 2][:], ACT.Tanh, scale=0.5).then_inc(ze_s.sem, 1)

                def gate_tanh(n):
                    dense_ready(act, T_HEAD, HEAD_TILES, i, 4 + n)
                    act.wait_ge(gate_st[n % 2].sem, gate_st[n % 2].at(i, 16 * (n // 2)))
                    if n == 1:
                        act.wait_ge(z_s.sem, z_s.at(i, 2))
                    nc.scalar.activation(gate_o[n % 2], dense_b[(T_HEAD + n) % 2][:], ACT.Tanh, scale=0.5)\
                        .then_inc(gate_s.sem, 1)

                def vn_copy(c):
                    act.wait_ge(vn_p.sem, vn_p.at(i, c + 1))
                    if c:
                        act.wait_ge(up_p.sem, up_p.at(i, c))
                    nc.scalar.copy(v_new, g0[:, 0:P]).then_inc(vn_s.sem, 1)

                act.wait_ge(dg_s.sem, dg_s.at(i, 4))
                nc.scalar.activation(e_mat, dg, ACT.Exp).then_inc(e_s.sem, 1)
                nc.scalar.activation(e_g, g_bc, ACT.Exp).then_inc(eg_s.sem, 1)
                hi(1, 0, 1, 2)
                act.wait_ge(on_p.sem, on_p.at(i, 0))
                w_copy(1)
                hi(1, 3)
                hi(2, 0)
                act.wait_ge(qn_p.sem, qn_p.at(i, 1))
                act.wait_ge(o_st.sem, o_st.at(i, 0))
                nc.scalar.copy(q_n, a0[:]).then_inc(qn_s.sem, 1)
                act.wait_ge(vconv_s.sem, vconv_s.at(i, 4))
                nc.scalar.activation(v_e, v_conv, ACT.Tanh, scale=0.5).then_inc(vtanh_s.sem, 1)
                w_copy(2)
                hi(2, 1)
                act.wait_ge(kn_p.sem, kn_p.at(i, 1))
                nc.scalar.copy(k_n, a0[:]).then_inc(kn_s.sem, 1)
                hi(2, 2)
                dense_ready(act, T_HEAD, HEAD_TILES, i, 1)
                nc.scalar.copy(v_tok, a1[:]).then_inc(vt_s.sem, 1)
                hi(2, 3)
                hi(3, 0)
                w_copy(3)
                hi(3, 1, 2)
                for j in range(2):
                    act.wait_ge(qk_stored[j].sem, qk_stored[j].at(NH - 1, 16))
                exp_scores(0)
                w_copy(4)
                hi(3, 3)
                exp_scores(1)
                z_tanh(0, 2)
                hi(4, 0)
                w_copy(5)
                pt_copy(0)
                hi(4, 1)
                exp_scores(2)
                pt_copy(1)
                hi(4, 2)
                exp_scores(3)
                hi(4, 3)
                act.wait_ge(tt_s.sem, tt_s.at(i, 1))
                nc.scalar.copy(t_mat, g1[:]).then_inc(ttc_s.sem, 1)
                z_tanh(1, 3)
                w_copy(6)
                pt_copy(2)
                hi(5, 0)
                pt_copy(3)
                hi(5, 1)
                vn_copy(0)
                hi(5, 2, 3)
                gate_tanh(0)
                hi(6, 0)
                vn_copy(1)
                hi(6, 1, 2, 3)
                gate_tanh(1)
                vn_copy(2)
                hi(7, 0, 1, 2, 3)
                vn_copy(3)
                gate_tanh(2)
                hi(8, 0)
                act.wait_ge(o_p.sem, o_p.at(i, 1))
                nc.scalar.activation(o_sq, o_bank[:], ACT.Square).then_inc(osq_s.sem, 1)
                hi(8, 1)
                act.wait_ge(on_p.sem, on_p.at(i, 1))
                nc.scalar.activation(o_ln, misc[:], ACT.Ln, bias=eps, scale=1.0 / P).then_inc(oln_s.sem, 1)
                act.wait_ge(oln_s.sem, oln_s.at(i, 1))
                nc.scalar.activation(o_rs, o_ln, ACT.Exp, scale=-0.5).then_inc(ors_s.sem, 1)
                hi(8, 2, 3)
                gate_tanh(3)

            for n in range(2 * NH):
                act.wait_ge(o_in_s[n % N_O], 16 * (n // N_O + 1))
                act.wait_ge(dense_done, 4 * (T_MERGE - 1) + n // 4 + 1)
                nc.scalar.copy(h_hi[:, n, :], o_in[:, n % N_O, :]).then_inc(oh_s, 1)

            with act.Fori(0, KT // 2) as i:
                for j in range(2):
                    for q in range(4):
                        split_hi(act, T_MERGE, 2, i, j + 1, q)
                    act.wait_ge(ym_s.sem, ym_s.at(i, j + 1))
                    nc.scalar.copy(m_hi[:, bass.ds(i * 2 + j, 1), :], ym[:].unsqueeze(1)).then_inc(mh_s, 1)

            def out_turn(i, last):
                for j in range(4):
                    if not (last and j == 3):
                        for q in range(4):
                            split_hi(act, T_OUT, 4, i, j + 1, q)
                for c in range(NCH):
                    act.wait_ge(y_add[c].sem, y_add[c].at(i, 1))
                    act.wait_ge(ysq_s.sem, ysq_s.at(i, c))
                    nc.scalar.activation(ysq[:], y[:, c, bass.ds(i * SEQ, SEQ)], ACT.Square,
                                         accum_out=ssum[:, c, bass.ds(i, 1)]).then_inc(ysq_s.sem, 1)
                    if last:
                        final_norm(c)

            def final_norm(c):
                act.wait_ge(fin_v, c + 1)
                nc.scalar.activation(stot[:, c, 1:2], stot[:, c, 0:1], ACT.Ln, bias=eps, scale=1.0 / D_MODEL).then_inc(fin_a, 1)
                act.wait_ge(fin_a, 2 * c + 1)
                nc.scalar.activation(stot[:, c, 2:3], stot[:, c, 1:2], ACT.Exp, scale=-0.5).then_inc(fin_a, 1)
                act.wait_ge(fin_a, 2 * c + 2)
                act.wait_ge(yw_s, 12)
                nc.scalar.activation(y[:, c, 0:HALF], y[:, c, 0:HALF], ACT.Copy, scale=stot[:, c, 2:3]).then_inc(yn_a, 1)

            nc.scalar.preload_act_table_set("natural_log_exp_and_others")
            with act.Fori(0, 3) as i:
                out_turn(i, False)
            out_turn(3, True)

        @block.vector
        def _(dve):
            for n in range(KT // 2):
                dve.wait_ge(x_in[n], 16)
                if n >= 2:
                    dve.wait_ge(xsum_done, n - 1)
                nc.vector.tensor_tensor(x_sq2[n % 2], xs[2 * n + 1], xs[2 * n + 1], ALU.mult).then_inc(xsq_v, 1)
                dve.wait_ge(xsq_v, n + 1)
                dve.wait_ge(xsq_done, n + 1)
                nc.vector.tensor_tensor(x_sq2[n % 2], x_sq2[n % 2], x_sq[n % 2], ALU.add).then_inc(xpair_done, 1)
            dve.wait_ge(param_in, 16)
            dve.wait_ge(const_in, 16)

            def h_scaled(k):
                if k == 0:
                    dve.wait_ge(xrs_done, 2)
                if k >= 2:
                    dve.wait_ge(hl_done, k - 1)
                nc.vector.scalar_tensor_tensor(h_tmp[k % 2], xs[k], param[:, P_NORM + k:P_NORM + k + 1], x_rs,
                                               ALU.mult, ALU.mult).then_inc(hm_done, 1)

            def h_low(k):
                dve.wait_ge(hh_done, k + 1)
                nc.vector.tensor_tensor(h_lo[:, k, :], h_tmp[k % 2], h_hi[:, k, :].bitcast(F32),
                                        ALU.subtract).then_inc(hl_done, 1)

            for k in range(KT):
                h_scaled(k)
                if k >= 1:
                    h_low(k - 1)
            h_low(KT - 1)
            dve.wait_ge(lo_done, 8)
            for q in range(4):
                split_lo(dve, 0, 2, 0, 2, q)
            dve.wait_ge(mask_in, 16)
            nc.vector.tensor_copy(lmask[:].rearrange("p a n -> p (a n)"), mask_i).then_inc(mask_done, 1)

            dve.wait_ge(pos_in, 16)
            c1, c2, magic = 6.28125, float(np.float32(2 * math.pi - 6.28125)), 1.5 * 2.0 ** 23
            nc.vector.tensor_copy(pos_f, pos_i).then_inc(rope_v, 1)
            dve.wait_ge(rope_v, 1)
            nc.vector.tensor_scalar(ang, pos_f, const[:, C_FREQ:C_FREQ + 1], None, ALU.mult).then_inc(rope_v, 1)
            dve.wait_ge(rope_v, 2)
            nc.vector.tensor_scalar(turns, ang, 1.0 / (2 * math.pi), const[:, C_TURN:C_TURN + 1],
                                    ALU.mult, ALU.add).then_inc(rope_v, 1)
            dve.wait_ge(rope_v, 3)
            nc.vector.tensor_scalar(turns, turns, magic, -magic, ALU.add, ALU.add).then_inc(rope_v, 1)
            dve.wait_ge(rope_v, 4)
            nc.vector.scalar_tensor_tensor(ang, turns, -c1, ang, ALU.mult, ALU.add).then_inc(rope_v, 1)
            dve.wait_ge(rope_v, 5)
            nc.vector.scalar_tensor_tensor(ang, turns, -c2, ang, ALU.mult, ALU.add).then_inc(rope_v, 1)
            dve.wait_ge(rope_v, 6)
            nc.vector.tensor_scalar(ang, ang, const[:, C_TURN2PI:C_TURN2PI + 1], 3.141592, ALU.add, ALU.min)\
                .then_inc(rope_v, 1)
            dve.wait_ge(rope_v, 7)
            nc.vector.tensor_scalar(ang, ang, -3.141592, None, ALU.max).then_inc(rope_v, 1)
            for t in range(3, N_PRE + 1):
                for q in range(4):
                    split_lo(dve, 0, 2, 0, t, q)

            def c_scaled(j):
                n = 0 if j < CQ else 1
                dve.wait_ge(crs_done, 2 * n + 2)
                if j >= 2:
                    dve.wait_ge(cl_done, j - 1)
                nc.vector.scalar_tensor_tensor(c_tmp[j % 2], c_raw[j], param[:, P_QN + j:P_QN + j + 1], c_rs[n],
                                               ALU.mult, ALU.mult).then_inc(cm_done, 1)

            def c_low(j):
                dve.wait_ge(ch_done, j + 1)
                nc.vector.tensor_tensor(c_lo[:, j, :], c_tmp[j % 2], c_hi[:, j, :].bitcast(F32),
                                        ALU.subtract).then_inc(cl_done, 1)

            for j in range(CQ + CK):
                c_scaled(j)
                if j >= 1:
                    c_low(j - 1)
            c_low(CQ + CK - 1)

            heads, brows = slice(0, NH), slice(32, 32 + NH)
            dt_bias = param[heads, P_DT:P_DT + 1]
            dve.wait_ge(spec_done, 1)
            nc.vector.tensor_scalar(g_sp[heads, :], special[heads, :], dt_bias, None, ALU.add).then_inc(decay_v, 1)
            dve.wait_ge(decay_v, 1)
            nc.vector.scalar_tensor_tensor(g_abs[heads, :], g_sp[heads, :], -1.0, g_sp[heads, :], ALU.mult, ALU.max)\
                .then_inc(decay_v, 1)
            nc.vector.tensor_scalar(g_sp[heads, :], g_sp[heads, :], 0.0, None, ALU.max).then_inc(decay_v, 1)
            dve.wait_ge(decay_v, 3)
            dve.wait_ge(decay_a, 4)
            nc.vector.tensor_tensor(g_sp[heads, :], g_sp[heads, :], g_ln[heads, :], ALU.add).then_inc(decay_v, 1)
            dve.wait_ge(decay_v, 4)
            nc.vector.tensor_scalar(g_sp[heads, :], g_sp[heads, :], a_neg, -1.0, ALU.mult, ALU.mult).then_inc(decay_v, 1)
            nc.vector.memset(gb, 0.0).then_inc(decay_v, 1)
            dve.wait_ge(decay_v, 6)
            for c in range(NCH):
                sl = slice(c * P, (c + 1) * P)
                nc.vector.tensor_tensor_scan(gb[heads, sl], ones[heads, 0:P], g_sp[heads, sl], 0.0,
                                             ALU.mult, ALU.add).then_inc(decay_v, 1)
            nc.vector.tensor_scalar(gb[brows, :], g_ex[brows, :], 0.5, 0.5, ALU.mult, ALU.add).then_inc(decay_v, 1)

            def conv(src, dst, wcol, done, i_wait, n0):
                def tap(k):
                    return param[:, bass.ds(wcol + k, 1)] if not isinstance(wcol, int) else param[:, wcol + k:wcol + k + 1]
                nc.vector.tensor_scalar(dst, src[:], tap(3), None, ALU.mult).then_inc(done, 1)
                for s in range(1, 4):
                    dve.wait_ge(done, i_wait(n0 + s))
                    ins = nc.vector.scalar_tensor_tensor(dst[:, s:SEQ], src[:, 0:SEQ - s], tap(3 - s), dst[:, s:SEQ],
                                                         ALU.mult, ALU.add)
                    ins.then_inc(done, 1)

            def qk_conv(i, j):
                dense_ready(dve, T_QK, 2, i, j)
                if not (isinstance(i, int) and i == 0):
                    dve.wait_ge(cvs_done, i * 2 + (j - 1))
                conv(dense_b[(T_QK + j) % 2], cv[j], i * 4 + (P_CONV + 32 * j), conv_done, lambda n: i * 8 + n, 4 * j)

            def qk_silu(i, j):
                dve.wait_ge(cve_done, i * 2 + (j + 1))
                if not (isinstance(i, int) and i == 0):
                    dve.wait_ge(cvo_done, i * 2 + (j - 1))
                nc.vector.scalar_tensor_tensor(cv_s[j], cv_e[j], 1.0, cv[j], ALU.add, ALU.mult).then_inc(cvs_done, 1)

            def qk_norm(n, j, turn):
                dve.wait_ge(cvrs_done, n + 1)
                if turn is not None:
                    dve.wait_ge(qk_stored[j].sem, qk_stored[j].at(turn, 0))
                nc.vector.scalar_tensor_tensor(cv_o[j], cv_s[j], 0.5 * float(P) ** -0.5 if j == 0 else 0.5, cv_rs,
                                               ALU.mult, ALU.mult).then_inc(cvo_done, 1)

            def rope_key():
                dve.wait_ge(swap_done, 1)
                dve.wait_ge(cs_done, 1)
                nc.vector.tensor_tensor(k_x, misc[:], cs[:], ALU.mult).then_inc(kx_done, 1)
                dve.wait_ge(gbt_done, 1)
                gt = o_bank[:].rearrange("p (c n) -> p n c", c=NCH)
                nc.vector.tensor_scalar(gball[:, :, 0:4], gt[:, 0:NH, :], -1.0, None, ALU.mult).then_inc(gball_done, 1)
                nc.vector.tensor_scalar(gball[:, :, 4:8], gt[:, 32:32 + NH, :], 0.5, None, ALU.mult).then_inc(gball_done, 1)
                dve.wait_ge(fold_done, 1)
                nc.vector.tensor_copy(krope[:], a0[:]).then_inc(krope_done, 1)

            for q in range(4):
                split_lo(dve, T_QK, 2, 0, 1, q)
            rope_key()

            def qk_turn(i, last=False):
                first = isinstance(i, int) and i == 0
                for j in range(2):
                    def lo(*qs):
                        if not (last and j == 1):
                            for q in qs:
                                split_lo(dve, T_QK, 2, i, j + 2, q)
                    qk_conv(i, j)
                    lo(0)
                    if not (first and j == 0):
                        qk_norm(i * 2 + (j - 1), 1 - j, None if first else i if j else i - 1)
                    lo(1)
                    qk_silu(i, j)
                    lo(2, 3)

            qk_turn(0)
            with dve.Fori(1, NH - 1) as i:
                qk_turn(i)
            qk_turn(NH - 1, True)
            qk_norm(2 * NH - 1, 1, NH - 1)

            with dve.Fori(0, NH) as i:
                def lo(j, *qs):
                    for q in qs:
                        split_lo(dve, T_HEAD, HEAD_TILES, i, j, q)

                def w(s, n):
                    dve.wait_ge(s.sem, s.at(i, n))

                waiter = small[:, 40:41]

                def update(l):
                    w(y_s, l)
                    nc.vector.memset(waiter, 0.0)
                    nc.vector.copy_predicated(blocks(u_mat), lmask[:, l:l + 1, :].to_broadcast([P, NCH, P]),
                                              blocks(g0[:])).then_inc(u_s.sem, 1)
                    if l <= 4:
                        w(u_s, l + 2)
                        nc.vector.transpose(t_mat, u_mat).then_inc(t_s.sem, 1)

                def score_max(b):
                    n = (b + 1) * P
                    src = a0 if b % 2 == 0 else a1
                    w(sc_p, b + 1)
                    nc.vector.tensor_tensor(src[:, b * P:n], src[:, b * P:n], mask_q, ALU.add).then_inc(msk_s.sem, 1)
                    w(msk_s, b + 1)
                    nc.vector.reduce_max(sc_max[:, b:b + 1], src[:, 0:n], AX_X).then_inc(max_s.sem, 1)
                    w(max_s, b + 1)
                    nc.vector.tensor_scalar(sc_nb[:, b:b + 1], sc_max[:, b:b + 1], -SCALE, None, ALU.mult)\
                        .then_inc(nb_s.sem, 1)

                def normalise(b):
                    n = (b + 1) * P
                    w(ex_s, b + 1)
                    nc.vector.reciprocal(sc_r[:, b:b + 1], sc_sum[:, b:b + 1]).then_inc(rc_s.sem, 1)
                    w(rc_s, b + 1)
                    nc.vector.tensor_scalar(prob[b % 2][:, 0:n], prob[b % 2][:, 0:n], sc_r[:, b:b + 1], None, ALU.mult)\
                        .then_inc(pn_s.sem, 1)

                def z_silu(n, dst):
                    w(ze_s, n + 1)
                    nc.vector.scalar_tensor_tensor(dst, z_e, 1.0, dense_b[(T_HEAD + 2 + n) % 2][:], ALU.add, ALU.mult)\
                        .then_inc(z_s.sem, 1)

                def x_chunk(c):
                    w(ks_p, c)
                    if c >= 1:
                        w(vn_p, c)
                    nc.vector.tensor_tensor(x_c, v_beta[:, c * P:(c + 1) * P], g1[:, 0:P], ALU.subtract)\
                        .then_inc(x_s.sem, 1)

                def state_update(c):
                    w(up_p, c + 1)
                    if c == 0:
                        ins = nc.vector.tensor_copy(state, g1[:, 0:P])
                    else:
                        w(st_s, c)
                        ins = nc.vector.scalar_tensor_tensor(state, state, e_g[:, (c + 1) * P - 1:(c + 1) * P], g1[:, 0:P],
                                                             ALU.mult, ALU.add)
                    ins.then_inc(st_s.sem, 1)

                w(head_in, 64)
                w(o_p, 0)
                nc.vector.tensor_copy(hs, gball[:, bass.ds(i, 1), :].rearrange("p a n -> p (a n)")).then_inc(hs_s.sem, 1)
                w(hs_s, 1)
                for c in range(NCH):
                    sl = slice(c * P, (c + 1) * P)
                    nc.vector.scalar_tensor_tensor(dg[:, sl], g_bc[:, sl], hs[:, c:c + 1], mask_g, ALU.add, ALU.add)\
                        .then_inc(dg_s.sem, 1)
                w(oa_s, 0)
                nc.vector.tensor_tensor(kb, kh, b_bc, ALU.mult).then_inc(kb_s.sem, 1)
                w(kb_s, 1)
                w(eg_s, 1)
                nc.vector.tensor_tensor(kbe, kb, e_g, ALU.mult).then_inc(dec_s.sem, 1)
                nc.vector.tensor_tensor(qd, qh, e_g, ALU.mult).then_inc(dec_s.sem, 1)
                w(kk_s, 1)
                w(e_s, 1)
                nc.vector.scalar_tensor_tensor(nat, g0[:], -1.0, e_mat, ALU.mult, ALU.mult).then_inc(nat_s.sem, 1)
                nc.vector.tensor_copy(blocks(u_mat), ident.unsqueeze(1).to_broadcast([P, NCH, P])).then_inc(u_s.sem, 1)
                w(u_s, 1)
                w(nat_s, 1)
                nc.vector.memset(waiter, 0.0)
                nc.vector.copy_predicated(blocks(u_mat), lmask[:, 0:1, :].to_broadcast([P, NCH, P]),
                                          blocks(nat)).then_inc(u_s.sem, 1)
                w(u_s, 2)
                nc.vector.transpose(t_mat, u_mat).then_inc(t_s.sem, 1)
                w(ktr_s, 1)
                nc.vector.tensor_tensor(blocks(k_dec), blocks(misc[:]), blocks(e_mat)[:, :, P - 1:P].to_broadcast([P, NCH, P]),
                                        ALU.mult).then_inc(kdec_s.sem, 1)
                lo(1, 0, 1)
                w(qk_s, 1)
                nc.vector.tensor_tensor(attn, g0[:], e_mat, ALU.mult).then_inc(attn_s.sem, 1)
                lo(1, 2, 3)
                update(1)
                dense_ready(dve, T_HEAD, HEAD_TILES, i, 0)
                conv(dense_b[T_HEAD % 2], v_conv, i * 4 + (P_CONV + 64), vconv_s.sem, lambda n: vconv_s.at(i, n), 0)
                w(qx_p, 1)
                w(o_st, 0)
                nc.vector.tensor_tensor(q_x, a1[:], cs[:], ALU.mult).then_inc(qx_s.sem, 1)
                lo(2, 0)
                update(2)
                w(vtanh_s, 1)
                nc.vector.scalar_tensor_tensor(v_sil, v_e, 1.0, v_conv, ALU.add, ALU.mult).then_inc(vsil_s.sem, 1)
                lo(2, 1, 2, 3)
                lo(3, 0)
                update(3)
                w(vtr_s, 1)
                nc.vector.tensor_tensor(blocks(v_beta), blocks(misc[:]), hs[:, 4:8].unsqueeze(2).to_broadcast([P, NCH, P]),
                                        ALU.mult).then_inc(vb_s.sem, 1)
                lo(3, 1)
                score_max(0)
                lo(3, 2)
                normalise(0)
                score_max(1)
                lo(3, 3)
                update(4)
                z_silu(0, z_b)
                lo(4, 0)
                normalise(1)
                update(5)
                score_max(2)
                lo(4, 1)
                score_max(3)
                normalise(2)
                lo(4, 2)
                normalise(3)
                lo(4, 3)
                z_silu(1, z_a)
                update(6)
                lo(5, 0, 1)
                state_update(0)
                lo(5, 2)
                x_chunk(1)
                w(pv_p, 1)
                nc.vector.scalar_tensor_tensor(o_b, a0[:], 0.5, z_b, ALU.mult, ALU.mult).then_inc(ob_s.sem, 1)
                lo(5, 3)
                lo(6, 0)
                state_update(1)
                lo(6, 1)
                x_chunk(2)
                lo(6, 2, 3)
                state_update(2)
                lo(7, 0)
                x_chunk(3)
                lo(7, 1, 2, 3)
                lo(8, 0, 1)
                w(ors_s, 1)
                nc.vector.scalar_tensor_tensor(o_n, o_bank[:], param[:, P_GN:P_GN + 1], o_rs, ALU.mult, ALU.mult)\
                    .then_inc(on_s.sem, 1)
                w(on_s, 1)
                nc.vector.scalar_tensor_tensor(o_a, o_n, 0.5, z_a, ALU.mult, ALU.mult).then_inc(oa_s.sem, 1)
                lo(8, 2, 3)

            for n in range(2 * NH):
                dve.wait_ge(oh_s, n + 1)
                nc.vector.tensor_tensor(h_lo[:, n, :], o_in[:, n % N_O, :], h_hi[:, n, :].bitcast(F32), ALU.subtract)\
                    .then_inc(ol_s, 1)
            dve.wait_ge(ol_s, 2 * NH)

            with dve.Fori(0, KT // 2) as i:
                for j in range(2):
                    for q in range(4):
                        split_lo(dve, T_MERGE, 2, i, j + 1, q)
                    b = (T_MERGE + j) % 2
                    dense_ready(dve, T_MERGE, 2, i, j)
                    dve.wait_ge(gate_ld[j], i * 32 + 32)
                    dve.wait_ge(ym_s.sem, ym_s.at(i, j))
                    nc.vector.scalar_tensor_tensor(yb[:], gate_in[:, j, 0, :], 1.0, dense_b[b][:], ALU.add, ALU.mult).then_inc(ya_s[j].sem, 1)
                    nc.vector.scalar_tensor_tensor(ya[:], gate_in[:, j, 1, :], 1.0, (a0, a1)[b][:], ALU.add, ALU.mult).then_inc(ya_s[j].sem, 1)
                    dve.wait_ge(ya_s[j].sem, ya_s[j].at(i, 2))
                    dve.wait_ge(ml_s.sem, ml_s.at(i, j))
                    nc.vector.tensor_tensor(ym[:], ya[:], yb[:], ALU.add).then_inc(ym_s.sem, 1)
                    dve.wait_ge(mh_s, i * 2 + (j + 1))
                    nc.vector.tensor_tensor(m_lo[:, bass.ds(i * 2 + j, 1), :], ym[:].unsqueeze(1),
                                            m_hi[:, bass.ds(i * 2 + j, 1), :].bitcast(F32), ALU.subtract).then_inc(ml_s.sem, 1)

            tok_banks = [g0, g1, o_bank, misc]

            def out_turn(i, last):
                for j in range(4):
                    if not (last and j == 3):
                        for q in range(4):
                            split_lo(dve, T_OUT, 4, i, j + 1, q)
                for c in range(NCH):
                    dve.wait_ge(tok_p, i * 3 + (c + 1)) if c < NCH - 1 else dense_ready(dve, T_OUT, 4, i, 3)
                    dve.wait_ge(resid_in, 16)
                    cols = y[:, c, bass.ds(i * SEQ, SEQ)]
                    nc.vector.scalar_tensor_tensor(cols, tok_banks[c][:], 0.5, cols, ALU.mult, ALU.add).then_inc(y_add[c].sem, 1)
                    if last and c:
                        final_norm(c - 1)
                if last:
                    final_norm(NCH - 1)
                    return
                dve.wait_ge(wf_in, 16)
                for c in range(NCH):
                    dve.wait_ge(ysq_s.sem, ysq_s.at(i, c + 1))
                    cols = y[:, c, bass.ds(i * SEQ, SEQ)]
                    nc.vector.tensor_tensor(cols, cols, wf[:, bass.ds(i * SEQ, SEQ)], ALU.mult).then_inc(yw_s, 1)

            def final_norm(c):
                dve.wait_ge(ysq_s.sem, ysq_s.at(3, c + 1))
                nc.vector.reduce_sum(stot[:, c, 0:1], ssum[:, c, :], AX_X).then_inc(fin_v, 1)
                dve.wait_ge(fin_a, 2 * c + 2)
                dve.wait_ge(yw_s, 12)
                third, fourth = y[:, c, HALF:3 * SEQ], y[:, c, 3 * SEQ:D_MODEL]
                nc.vector.tensor_scalar(third, third, stot[:, c, 2:3], None, ALU.mult).then_inc(yn_s, 1)
                nc.vector.scalar_tensor_tensor(fourth, fourth, stot[:, c, 2:3], wf[:, 3 * SEQ:D_MODEL], ALU.mult, ALU.mult)\
                    .then_inc(yn_s, 1)

            with dve.Fori(0, 3) as i:
                out_turn(i, False)
            out_turn(3, True)

        @block.tensor
        def _(pe):
            mm = nc.tensor.matmul
            pe.wait_ge(const_in, 16)
            for n in range(KT // 2):
                pe.wait_ge(xpair_done, n + 1)
                mm(misc[:], ones, x_sq2[n % 2], start=n == 0, stop=n == KT // 2 - 1).then_inc(xsum_done, 1)

            def c_sum(j):
                pe.wait_ge(csq_done, j + 1)
                if j == 0:
                    pe.wait_ge(xrs_done, 1)
                dst = misc if j < CQ else o_bank
                mm(dst[:], ones, c_sq[j % 2], start=j in (0, CQ), stop=j in (CQ - 1, CQ + CK - 1)).then_inc(csum_done, 1)

            for q in range(4):
                for t in range(2):
                    split_wait(pe, 0, 2, 0, t, q)
                    for k in range(4 * q, 4 * q + 4):
                        if t == 0:
                            pe.wait_ge(hl_done, k + 1)
                        sl = slice(k * P, (k + 1) * P)
                        ins = three(dense_b[t][:], w_hi[t][:, sl], w_lo[t][:, sl], h_hi[:, k, :], h_lo[:, k, :],
                                    k == 0, k == KT - 1)
                    if q == 3:
                        ins.then_inc(dense_done, 4)
            for t in range(2, N_PRE):
                for q in range(4):
                    if q == 0:
                        pe.wait_ge(csq_done, t - 1)
                    dense(pe, 0, 2, 0, t, q)
                    if q == 0 and t == 2:
                        c_sum(0)
                    if q == 1:
                        c_sum(t - 1)

            def qk_sum(i, j):
                pe.wait_ge(cvq_done, i * 2 + (j + 1))
                if not (isinstance(i, int) and i == 0 and j == 0):
                    pe.wait_ge(cvln_done, i * 2 + j)
                mm(misc[:], ones, cv_q[j], start=True, stop=True).then_inc(cvsum_done, 1)

            for q in range(4):
                if q == 0:
                    pe.wait_ge(csq_done, CQ + CK)
                dense(pe, T_QK, 2, 0, 0, q)
            pe.wait_ge(spec_done, 1)
            pe.wait_ge(crs_done, 3)
            mm(misc[:], swap, special, start=True, stop=True).then_inc(swap_done, 1)
            pe.wait_ge(decay_v, 11)
            for c in range(NCH):
                last = nc.tensor.transpose(o_bank[:, c * P:c * P + P], gb[:, c * P:(c + 1) * P], ident)
            last.then_inc(gbt_done, 1)
            pe.wait_ge(kx_done, 1)
            mm(a0[:], fold, k_x, start=True, stop=True).then_inc(fold_done, 1)
            for q in range(4):
                if q == 0:
                    pe.wait_ge(spec_done, 1)
                dense(pe, T_QK, 2, 0, 1, q)
                if q == 2:
                    qk_sum(0, 0)
            with pe.Fori(1, NH) as i:
                for j in range(2):
                    for q in range(4):
                        if q == 0:
                            pe.wait_ge(conv_done, i * 8 + 4 * j - 4)
                        dense(pe, T_QK, 2, i, j, q)
                        if q == 2:
                            qk_sum(i - 1, 1) if j == 0 else qk_sum(i, 0)

            qk_sum(NH - 1, 1)

            with pe.Fori(0, NH) as i:
                def w(s, n):
                    pe.wait_ge(s.sem, s.at(i, n))

                def d(j, *qs):
                    for q in qs:
                        dense(pe, T_HEAD, HEAD_TILES, i, j, q)

                def chunk(ap, c):
                    return ap[:, c * P:(c + 1) * P]

                def level_w(l):
                    w(t_s, l) if l <= 5 else w(ttc_s, 1)
                    if l == 1:
                        w(x_s, 0)
                        w(nat_s, 1)
                    else:
                        w(wc_s, l - 1)
                    for c in range(NCH):
                        ins = mm(chunk(g1, c), chunk(nat, c), chunk(t_mat, c), start=True, stop=True)
                    ins.then_inc(w_s.sem, 1)

                def level_y(l):
                    w(wc_s, l)
                    w(u_s, l + 1)
                    if l == 1:
                        w(attn_s, 1)
                    for c in range(NCH):
                        ins = mm(chunk(g0, c), chunk(w_mat, c), chunk(u_mat, c), start=True, stop=True)
                    ins.then_inc(y_s.sem, 1)

                def scores(b):
                    n = (b + 1) * P
                    dst = a0 if b % 2 == 0 else a1
                    if b >= 2:
                        w(ex_s, b - 1)
                    mm(dst[:, 0:n], chunk(q_n, b), k_n[:, 0:n], start=True, stop=False)
                    mm(dst[:, 0:n], chunk(q_x, b), krope[:, 0:n], start=False, stop=True).then_inc(sc_p.sem, 1)

                def prob_t(b):
                    w(pn_s, b + 1)
                    if b == 0:
                        w(vb_s, 1)
                    else:
                        w(pt_s, b)
                    for n in range(b + 1):
                        ins = nc.tensor.transpose(chunk(misc, n), chunk(prob[b % 2], n), ident)
                    ins.then_inc(pt_p.sem, 1)

                def v_new_product(c):
                    if c == 0:
                        w(u_s, 8)
                        w(vb_s, 1)
                    else:
                        w(x_s, c)
                        w(vn_s, c)
                    rhs = chunk(v_beta, 0) if c == 0 else x_c
                    mm(g0[:, 0:P], chunk(u_mat, c), rhs, start=True, stop=True).then_inc(vn_p.sem, 1)

                def out_and_state(c):
                    w(vn_s, c + 1)
                    if c == 0:
                        w(on_s, 0)
                        w(wc_s, 6)
                    ins = mm(chunk(o_bank, c), v_new, chunk(attn, c), start=c == 0, stop=True)
                    if c == NCH - 1:
                        ins.then_inc(o_p.sem, 1)
                    if c < NCH - 1:
                        mm(g1[:, 0:P], chunk(k_dec, c), v_new, start=True, stop=True).then_inc(up_p.sem, 1)

                def k_state(c):
                    w(st_s, c)
                    mm(g1[:, 0:P], chunk(kbe, c), state, start=True, stop=True).then_inc(ks_p.sem, 1)
                    mm(chunk(o_bank, c), state, chunk(qd, c), start=True, stop=False)

                def up_project(dst, kts, col, c_first, ready, last_inc=None):
                    for n, k in enumerate(range(kts)):
                        sl = slice(col + 256 * k, col + 256 * k + P)
                        ins = three(dst[:], w_hi[ub][:, sl], w_lo[ub][:, sl], c_hi[:, c_first + k, :], c_lo[:, c_first + k, :],
                                    n == 0, n == kts - 1)
                    ins.then_inc(ready.sem, 1)

                ub = (T_HEAD + 1) % 2

                pe.wait_ge(conv_done, 8 * NH - 4)
                w(gate_s, -1)
                d(0, 0)
                w(head_in, 64)
                w(kb_s, 1)
                w(vn_s, 0)
                for c in range(NCH):
                    ins = mm(chunk(g0, c), chunk(kh, c), chunk(kb, c), start=True, stop=True)
                ins.then_inc(kk_s.sem, 1)
                w(oln_s, 0)
                pe.wait_ge(cvln_done, 2 * NH)
                for c in range(NCH):
                    ins = nc.tensor.transpose(chunk(misc, c), chunk(kh, c), ident)
                ins.then_inc(ktr_s.sem, 1)
                d(0, 1)
                w(nat_s, 1)
                for c in range(NCH):
                    ins = mm(chunk(g0, c), chunk(kh, c), chunk(qh, c), start=True, stop=True)
                ins.then_inc(qk_s.sem, 1)
                d(0, 2)
                level_w(1)
                d(0, 3)
                level_y(1)
                split_wait(pe, T_HEAD, HEAD_TILES, i, 1, 3)
                pe.wait_ge(krope_done, 1)
                w(ob_s, 0)
                up_project(a0, CQ, 0, 0, qn_p)
                w(ex_s, 0)
                up_project(a1, CQ, P, 0, qx_p)
                level_w(2)
                w(qn_s, 1)
                up_project(a0, CK, 4 * 256, CQ, kn_p)
                level_y(2)
                w(qx_s, 1)
                for c in range(NCH):
                    for k in range(CK):
                        sl, tok = slice(1024 + 256 * k + P, 1024 + 256 * k + 2 * P), slice(c * P, (c + 1) * P)
                        mm(chunk(a1, c), c_hi[:, CQ + k, tok], w_hi[ub][:, sl], start=k == 0, stop=False)
                        mm(chunk(a1, c), c_lo[:, CQ + k, tok], w_hi[ub][:, sl], start=False, stop=False)
                        ins = mm(chunk(a1, c), c_hi[:, CQ + k, tok], w_lo[ub][:, sl], start=False, stop=k == CK - 1)
                    if c == NCH - 1:
                        ins.then_inc(dense_done, 4)
                w(vconv_s, 4)
                d(2, 0)
                level_w(3)
                d(2, 1)
                level_y(3)
                w(vsil_s, 1)
                w(kdec_s, 1)
                for c in range(NCH):
                    ins = nc.tensor.transpose(chunk(misc, c), chunk(v_sil, c), ident)
                ins.then_inc(vtr_s.sem, 1)
                w(kn_s, 1)
                scores(0)
                d(2, 2)
                level_w(4)
                w(vt_s, 1)
                scores(1)
                d(2, 3)
                level_y(4)
                pe.wait_ge(conv_done, 8 * NH)
                w(gate_s, 0)
                d(3, 0)
                level_w(5)
                prob_t(0)
                scores(2)
                d(3, 1)
                level_y(5)
                prob_t(1)
                scores(3)
                d(3, 2)
                w(u_s, 7)
                w(wc_s, 5)
                for c in range(NCH):
                    ins = nc.tensor.transpose(chunk(g1, c), chunk(u_mat, c), ident)
                ins.then_inc(tt_s.sem, 1)
                d(3, 3)
                level_w(6)
                prob_t(2)
                w(z_s, 1)
                d(4, 0)
                level_y(6)
                prob_t(3)
                d(4, 1)
                v_new_product(0)
                w(pt_s, 4)
                w(ex_s, 3)
                for n in range(NCH):
                    ins = mm(a0[:, n * P:SEQ], chunk(v_tok, n), p_t[:, n, n * P:SEQ], start=n == 0, stop=n == NCH - 1)
                ins.then_inc(pv_p.sem, 1)
                d(4, 2)
                out_and_state(0)
                d(4, 3)
                k_state(1)
                w(z_s, 2)
                d(5, 0)
                v_new_product(1)
                d(5, 1)
                out_and_state(1)
                d(5, 2)
                k_state(2)
                d(5, 3)
                v_new_product(2)
                w(gate_s, 1)
                d(6, 0)
                out_and_state(2)
                d(6, 1)
                k_state(3)
                d(6, 2)
                v_new_product(3)
                d(6, 3)
                out_and_state(3)
                w(gate_s, 2)
                d(7, 0, 1)
                w(osq_s, 1)
                mm(misc[:], ones, o_sq, start=True, stop=True).then_inc(on_p.sem, 1)
                d(7, 2, 3)

            pe.wait_ge(gate_s.sem, gate_s.at(NH - 1, 4))
            with pe.Fori(0, KT // 2) as i:
                for j in range(2):
                    b = (T_MERGE + j) % 2
                    pe.wait_ge(ya_s[j].sem, ya_s[j].at(i, 0))
                    for q in range(4):
                        split_wait(pe, T_MERGE, 2, i, j, q)
                        dst = dense_b[b] if q < 2 else (a0, a1)[b]
                        for k in range(4 * q, 4 * q + 4):
                            if j == 0:
                                pe.wait_ge(ol_s, k + 1)
                            sl = slice(k * P, (k + 1) * P)
                            ins = three(dst[:], w_hi[b][:, sl], w_lo[b][:, sl], h_hi[:, k, :], h_lo[:, k, :],
                                        k % 8 == 0, k % 8 == 7)
                        ins.then_inc(dense_done, 1)

            tok_banks = [g0, g1, o_bank, misc]
            pe.wait_ge(oln_s.sem, oln_s.at(NH - 1, 1))
            pe.wait_ge(on_s.sem, on_s.at(NH - 1, 1))
            pe.wait_ge(x_s.sem, x_s.at(NH - 1, 3))
            pe.wait_ge(vn_s.sem, vn_s.at(NH - 1, 4))
            with pe.Fori(0, 4) as i:
                for j in range(4):
                    b = (T_OUT + j) % 2
                    split_wait(pe, T_OUT, 4, i, j, 3)
                    pe.wait_ge(ml_s.sem, ml_s.base + 4 * j + 4)
                    for c in range(NCH):
                        if j == 0:
                            pe.wait_ge(y_add[c].sem, y_add[c].at(i, 0))
                        for k in range(4):
                            r, tok, sl = 4 * j + k, slice(c * P, (c + 1) * P), slice(k * SEQ, (k + 1) * SEQ)
                            last = c == NCH - 1
                            ins = [mm(tok_banks[c][:], m_hi[:, r, tok], w_hi[b][:, sl], start=r == 0, stop=False),
                                   mm(tok_banks[c][:], m_hi[:, r, tok], w_lo[b][:, sl], start=False, stop=False),
                                   mm(tok_banks[c][:], m_lo[:, r, tok], w_hi[b][:, sl], start=False, stop=r == KT - 1)]
                            if j == 3 and k == 3 and not last:
                                ins[2].then_inc(tok_p, 1)
                    ins[2].then_inc(dense_done, 4)


def weight_tiles(w_in, w_uq, w_ukv, proj_a, proj_b, w_out):
    def rows(w):
        return w.reshape(-1, P, w.shape[1]).transpose(1, 0, 2)

    at = np.cumsum([0, 3 * NH * P, NH * P, NH, NH, Q_RANK, KV_RANK, ROPE, NH * P, D_MODEL])
    qkv, z_a, alpha, beta, c_q, c_kv, k_rope, z_b, gates = (int(n) for n in at[:9])

    def columns(c0):
        return w_in[:, c0:c0 + P]

    special = np.zeros((D_MODEL, P), w_in.dtype)
    special[:, 0:NH] = w_in[:, alpha:alpha + NH]
    special[:, 32:32 + NH] = w_in[:, beta:beta + NH]
    special[:, 64:64 + ROPE] = w_in[:, k_rope:k_rope + ROPE]
    tiles = [rows(columns(c_q + n * P)) for n in range(CQ)] + [rows(columns(c_kv + n * P)) for n in range(CK)]
    tiles.append(rows(special))
    for h in range(NH):
        tiles += [rows(columns(qkv + h * P)), rows(columns(qkv + (NH + h) * P))]
    for h in range(NH):
        u = w_uq[:, h * 192:(h + 1) * 192]
        x1, x2 = u[:, P:P + 32], u[:, P + 32:P + 64]
        uq = rows(np.concatenate([u[:, 0:P], x1, x2, x2, x1], axis=1)).reshape(P, -1)
        ukv = rows(w_ukv[:, h * 256:(h + 1) * 256]).reshape(P, -1)
        pad = np.zeros((P, TILE - uq.shape[1] - ukv.shape[1]), w_in.dtype)
        tiles.append(rows(columns(qkv + (2 * NH + h) * P)))
        tiles.append(np.concatenate([uq, ukv, pad], axis=1))
        tiles += [rows(columns(z_b + h * P)), rows(columns(z_a + h * P))]
        tiles += [rows(columns(gates + (4 * h + n) * P)) for n in range(4)]
    for f in range(KT):
        sl = slice(f * P, (f + 1) * P)
        tiles.append(np.concatenate([rows(proj_b[:, sl]), rows(proj_a[:, sl])], axis=1))
    for n in range(4):
        for g in range(4):
            tiles.append(rows(w_out[g * SEQ:(g + 1) * SEQ, n * SEQ:(n + 1) * SEQ]))
    return np.ascontiguousarray(np.stack([t.reshape(P, TILE) for t in tiles]))


def constants():
    p = np.arange(P)
    c = np.zeros((P, N_CONST), np.float32)
    c[:, C_IDENT:C_IDENT + P] = np.eye(P)
    for n in range(ROPE):
        c[64 + n, C_SWAP + n] = 1
        c[64 + n, C_SWAP + 64 + (n + 32) % 64] = 1
    c[:, C_FOLD:C_FOLD + P] = p[:, None] % 64 == p[None, :] % 64
    c[:, C_ONES:C_ONES + P] = 1
    c[:, C_MASKQ:C_MASKQ + P] = np.where(p[None, :] <= p[:, None], 0, NEG)
    c[:, C_MASKG:C_MASKG + P] = np.where(p[None, :] >= p[:, None], 0, NEG)
    c[:, C_FREQ] = (10000.0 ** (-np.arange(0, ROPE, 2) / ROPE))[p % 32]
    turn = np.array([0.25, 0.25, 0.5, 0.0])[p // 32]
    c[:, C_TURN], c[:, C_TURN2PI], c[:, C_EPS] = turn, turn * 2 * math.pi, EPS
    m = np.zeros((P, 7, P), np.int32)
    j, i = p[:, None], p[None, :]
    for n in range(7):
        b = 1 << n
        m[:, n, :] = (i // (2 * b) == j // (2 * b)) & (i // b == j // b + 1)
    return c, m.reshape(P, 7 * P)


def kernel(x, positions, norm_w, w_in, conv_w, a_log, dt_bias, gdn_norm_w, q_norm_w, w_uq, kv_norm_w,
           w_ukv, proj_a, proj_b, w_out, final_norm_w):
    import concourse.bacc as bacc
    from concourse.bass_utils import run_bass_kernel_spmd

    (x, positions, norm_w, w_in, conv_w, a_log, dt_bias, gdn_norm_w, q_norm_w, w_uq, kv_norm_w, w_ukv, proj_a,
     proj_b, w_out, final_norm_w) = (np.asarray(a) for a in (
         x, positions, norm_w, w_in, conv_w, a_log, dt_bias, gdn_norm_w, q_norm_w, w_uq, kv_norm_w, w_ukv, proj_a,
         proj_b, w_out, final_norm_w))
    xs = np.ascontiguousarray(x[0])
    params = np.zeros((P, N_PARAM), np.float32)
    params[:, P_NORM:P_NORM + KT] = norm_w[0].reshape(KT, P).T
    params[:, P_QN:P_QN + CQ] = q_norm_w[0].reshape(CQ, P).T
    params[:, P_KVN:P_KVN + CK] = kv_norm_w[0].reshape(CK, P).T
    params[:, P_GN] = gdn_norm_w[0]
    params[:, P_CONV:P_CONV + 96] = conv_w[0].reshape(4, 24, P).transpose(2, 1, 0).reshape(P, 96)
    params[0:NH, P_DT], params[0:NH, P_ALOG] = dt_bias[0], a_log[0]
    consts, masks = constants()
    arrays = {
        "xt": np.ascontiguousarray(xs.T.reshape(KT, P, SEQ).transpose(1, 0, 2)),
        "x": xs, "positions": np.ascontiguousarray(positions), "params": params,
        "wfinal": final_norm_w.reshape(1, D_MODEL),
        "stream": weight_tiles(w_in[0], w_uq[0], w_ukv[0], proj_a[0], proj_b[0], w_out[0]),
        "consts": consts, "masks": masks,
    }
    nc = bacc.Bacc("TRN2", target_bir_lowering=False, num_devices=1)
    aps = {n: nc.dram_tensor(f"in_{n}", a.shape, mybir.dt.from_np(a.dtype), kind="ExternalInput").ap()
           for n, a in arrays.items()}
    out = nc.dram_tensor("out", (SEQ, D_MODEL), F32, kind="ExternalOutput").ap()
    program(nc, **aps, out=out)
    r = run_bass_kernel_spmd(nc, [{f"in_{n}": a for n, a in arrays.items()}], core_ids=[0])
    return r.results[0]["out"].reshape(1, SEQ, D_MODEL)
```
